# Optimizing a Trainium2 kernel written in Bass

```python
import functools
import jax, jax.numpy as jnp
from jax import lax
import numpy as np

'''One inference step of a hybrid causal decoder trunk (DEPTH layers) serving a prompt group and a
sample group with the SAME weights.

Per layer (pre-norm, plain residuals):
  h = RMSNorm(x);  [u, Bg, Cg, q/k/v per head group, g_a, g_b] = h @ w_in   (one combined projection)
  A = W_conv_out( Bg * dwconv3_causal( Cg * u ) )                          (short gated convolution)
  B = W_attn_out( merge_g softmax-attn_g(q_g, k_g, v_g) )                    (dilated sliding-window attention)
      head groups (window, dilation) = (128,1), (512,4), (2048,16), 4 heads x 128 each, rotary on q/k;
      a query at t reads keys at t, t-d, t-2d, ..., t-window (gathered by stride); the three groups'
      outputs are combined per head slot weighted by their softmax denominators (LongNet).
  x = x + W_o( sigmoid(g_a) * A + sigmoid(g_b) * B )
  [up, gate] = RMSNorm(x) @ w_ffn_in;  x = x + W_down( silu(dwconv3_causal(gate) + b) * up )   (ConvFFN)
final RMSNorm.

Inputs:
  x_prompt (BATCH, SEQ, D_MODEL) at positions 0..SEQ-1
  x_sample (DEC_BATCH, DEC_SEQ, D_MODEL) at positions PAST_LEN..PAST_LEN+DEC_SEQ-1
  cache_kv_g{1,2,3} (DEPTH, DEC_BATCH, min(W_g, PAST_LEN), 2, HEADS_PER_GROUP, HEAD_DIM): rotated keys and
      values of the last min(W_g, PAST_LEN) positions, oldest first (W_g = 128, 512, 2048)
  state_conv_mix (DEPTH, DEC_BATCH, CONV_W-1, D_CONV): last 2 inputs Cg*u of the short convolution
  state_conv_ffn (DEPTH, DEC_BATCH, CONV_W-1, D_FF): last 2 up-projected gate rows of the ConvFFN
Output tuple:
  (y_prompt (BATCH, SEQ, D_MODEL), y_sample (DEC_BATCH, DEC_SEQ, D_MODEL),
   p_kv_g1 (DEPTH, BATCH, min(128,SEQ), 2, 4, 128), p_kv_g2 (DEPTH, BATCH, min(512,SEQ), 2, 4, 128),
   p_kv_g3 (DEPTH, BATCH, min(2048,SEQ), 2, 4, 128), p_conv_mix (DEPTH, BATCH, 2, D_CONV),
   p_conv_ffn (DEPTH, BATCH, 2, D_FF),
   s_kv_g1 / s_kv_g2 / s_kv_g3 (DEPTH, DEC_BATCH, min(W_g, PAST_LEN), 2, 4, 128) updated window buffers,
   s_conv_mix (DEPTH, DEC_BATCH, 2, D_CONV), s_conv_ffn (DEPTH, DEC_BATCH, 2, D_FF))
'''

D_MODEL = 2048
BATCH = 1
SEQ = 256
DEPTH = 1
DEC_BATCH = 8
DEC_SEQ = 1
PAST_LEN = 256
PAGE_SIZE = 128

HEAD_DIM = 128
HEADS_PER_GROUP = 4
GROUPS = ((128, 1), (512, 4), (2048, 16))
N_GROUPS = len(GROUPS)
SUB_WIN = 128
ATT_W = HEADS_PER_GROUP * HEAD_DIM
ATT_SCALE = HEAD_DIM ** -0.5
D_CONV = D_MODEL // 2
CONV_W = 3
D_FF = 5632
ROPE_THETA = 10000.0
EPS = 1e-6
IN_SIZES = (D_CONV,) * 3 + (ATT_W,) * (3 * N_GROUPS) + (D_MODEL,) * 2
D_IN_PROJ = sum(IN_SIZES)
IN_SPLITS = tuple(int(s) for s in np.cumsum(IN_SIZES)[:-1])

kernel_name = 'hybrid_shortconv_dilated_swa_decoder_step'

def rmsnorm(x, g):
    xf = x.astype(jnp.float32)
    r = lax.rsqrt(jnp.mean(xf * xf, axis=-1, keepdims=True) + EPS)
    return (xf * r).astype(x.dtype) * g

def rope_angles(pos):
    half = HEAD_DIM // 2
    inv = ROPE_THETA ** (-jnp.arange(half, dtype=jnp.float32) / half)
    ang = pos.astype(jnp.float32)[:, None] * inv[None, :]
    return jnp.cos(ang)[None, :, None, :], jnp.sin(ang)[None, :, None, :]

def rope(x, cos, sin):
    half = HEAD_DIM // 2
    xf = x.astype(jnp.float32)
    x1, x2 = xf[..., :half], xf[..., half:]
    return jnp.concatenate([x1 * cos - x2 * sin, x2 * cos + x1 * sin], axis=-1).astype(x.dtype)

def causal_dwconv(u, prev, w):
    t = u.shape[1]
    xp = jnp.concatenate([prev.astype(u.dtype), u], axis=1)
    y = w[0] * xp[:, 0:t]
    for j in range(1, CONV_W):
        y = y + w[j] * xp[:, j:j + t]
    return y, xp[:, -(CONV_W - 1):]

def band_attention(q, k, v):
    n, L, h, d = q.shape
    nb = L // SUB_WIN
    qb = q.reshape(n, nb, SUB_WIN, h, d)
    kb = k.reshape(n, nb, SUB_WIN, h, d)
    vb = v.reshape(n, nb, SUB_WIN, h, d)

    def with_prev(a):
        prev = jnp.pad(a, ((0, 0), (1, 0), (0, 0), (0, 0), (0, 0)))[:, :-1]
        return jnp.concatenate([prev, a], axis=2)

    kk, vv = with_prev(kb), with_prev(vb)
    s = jnp.einsum('nbqhd,nbkhd->nbqhk', qb, kk, preferred_element_type=jnp.float32) * ATT_SCALE
    qi = jnp.arange(SUB_WIN)[:, None]
    kj = jnp.arange(2 * SUB_WIN)[None, :]
    band = (kj >= qi) & (kj <= qi + SUB_WIN)
    has_prev = jnp.arange(nb)[:, None, None] > 0
    mask = band[None] & (has_prev | (kj >= SUB_WIN)[None])
    s = jnp.where(mask[None, :, :, None, :], s, -jnp.inf)
    m = s.max(axis=-1)
    p = jnp.exp(s - m[..., None])
    den = p.sum(axis=-1)
    num = jnp.einsum('nbqhk,nbkhd->nbqhd', p.astype(v.dtype), vv, preferred_element_type=jnp.float32)
    return num.reshape(n, L, h, d), m.reshape(n, L, h), den.reshape(n, L, h)

def dilated_prompt(q, k, v, dil):
    b, t, h, d = q.shape
    span = dil * SUB_WIN
    t_pad = -(-t // span) * span
    sub_len = t_pad // dil

    def regroup(a):
        a = jnp.pad(a, ((0, 0), (0, t_pad - t), (0, 0), (0, 0)))
        a = a.reshape(b, sub_len, dil, h, d).transpose(0, 2, 1, 3, 4)
        return a.reshape(b * dil, sub_len, h, d)

    def ungroup(a):
        a = a.reshape((b, dil, sub_len) + a.shape[2:])
        a = jnp.moveaxis(a, 1, 2).reshape((b, t_pad) + a.shape[3:])
        return a[:, :t]

    num, m, den = band_attention(regroup(q), regroup(k), regroup(v))
    return ungroup(num), ungroup(m), ungroup(den)

def dilated_sample(q, k, v, kv_buf, dil):
    s_len = q.shape[1]
    w_eff = kv_buf.shape[1]
    kv_all = jnp.concatenate([kv_buf, jnp.stack([k, v], axis=2).astype(kv_buf.dtype)], axis=1)
    idx = w_eff + jnp.arange(s_len)[:, None] - dil * jnp.arange(SUB_WIN + 1)[None, :]
    valid = idx >= 0
    kv_g = jnp.take(kv_all, jnp.maximum(idx, 0), axis=1)
    sc = jnp.einsum('bshd,bsjhd->bshj', q, kv_g[:, :, :, 0], preferred_element_type=jnp.float32) * ATT_SCALE
    sc = jnp.where(valid[None, :, None, :], sc, -jnp.inf)
    m = sc.max(axis=-1)
    p = jnp.exp(sc - m[..., None])
    den = p.sum(axis=-1)
    num = jnp.einsum('bshj,bsjhd->bshd', p.astype(v.dtype), kv_g[:, :, :, 1], preferred_element_type=jnp.float32)
    return (num, m, den), kv_all[:, -w_eff:]

def merge_groups(outs, dtype):
    nums = jnp.stack([o[0] for o in outs])
    ms = jnp.stack([o[1] for o in outs])
    dens = jnp.stack([o[2] for o in outs])
    wts = jnp.exp(ms - ms.max(axis=0, keepdims=True))
    out = (wts[..., None] * nums).sum(axis=0) / (wts * dens).sum(axis=0)[..., None]
    return out.astype(dtype)

def attend_prompt(qs, ks, vs):
    outs, states = [], []
    for (win, dil), q, k, v in zip(GROUPS, qs, ks, vs):
        outs.append(dilated_prompt(q, k, v, dil))
        states.append(jnp.stack([k, v], axis=2)[:, -min(win, k.shape[1]):])
    return merge_groups(outs, qs[0].dtype), states

def attend_sample(qs, ks, vs, bufs):
    outs, states = [], []
    for (win, dil), q, k, v, buf in zip(GROUPS, qs, ks, vs, bufs):
        o, new_buf = dilated_sample(q, k, v, buf, dil)
        outs.append(o)
        states.append(new_buf)
    return merge_groups(outs, qs[0].dtype), states

def decoder_layer(x, pos, conv_prev, ffn_prev, attend, norm_mix, w_in, conv_mix_w, w_conv_out,
                  w_attn_out, w_out, norm_ffn, w_ffn_in, ffn_conv_w, ffn_conv_b, w_ffn_down):
    n, t, _ = x.shape
    h = rmsnorm(x, norm_mix)
    parts = jnp.split(h @ w_in, IN_SPLITS, axis=-1)
    u, b_gate, c_gate = parts[0], parts[1], parts[2]
    gate_a, gate_b = parts[-2], parts[-1]
    conv_y, conv_state = causal_dwconv(c_gate * u, conv_prev, conv_mix_w)
    branch_a = (b_gate * conv_y) @ w_conv_out
    cos, sin = rope_angles(pos)

    def heads(a):
        return a.reshape(n, t, HEADS_PER_GROUP, HEAD_DIM)

    qs = [rope(heads(parts[3 + 3 * g]), cos, sin) for g in range(N_GROUPS)]
    ks = [rope(heads(parts[4 + 3 * g]), cos, sin) for g in range(N_GROUPS)]
    vs = [heads(parts[5 + 3 * g]) for g in range(N_GROUPS)]
    att, kv_states = attend(qs, ks, vs)
    branch_b = att.reshape(n, t, ATT_W) @ w_attn_out
    x = x + (jax.nn.sigmoid(gate_a) * branch_a + jax.nn.sigmoid(gate_b) * branch_b) @ w_out
    h = rmsnorm(x, norm_ffn)
    up, gate = jnp.split(h @ w_ffn_in, 2, axis=-1)
    gate, ffn_state = causal_dwconv(gate, ffn_prev, ffn_conv_w)
    x = x + (jax.nn.silu(gate + ffn_conv_b) * up) @ w_ffn_down
    return x, conv_state, ffn_state, kv_states

def setup_inputs(seed: int = 0) -> dict:
    key = jax.random.key(seed)
    ks = jax.random.split(key, 20)
    f32 = jnp.float32

    def nrm(k, shape, scale):
        return jax.random.normal(k, shape, f32) * scale

    w_eff = [min(win, PAST_LEN) for win, _ in GROUPS]
    kv_shape = lambda w: (DEPTH, DEC_BATCH, w, 2, HEADS_PER_GROUP, HEAD_DIM)
    return {
        'x_prompt': nrm(ks[0], (BATCH, SEQ, D_MODEL), 1.0),
        'x_sample': nrm(ks[1], (DEC_BATCH, DEC_SEQ, D_MODEL), 1.0),
        'cache_kv_g1': nrm(ks[2], kv_shape(w_eff[0]), 1.0),
        'cache_kv_g2': nrm(ks[3], kv_shape(w_eff[1]), 1.0),
        'cache_kv_g3': nrm(ks[4], kv_shape(w_eff[2]), 1.0),
        'state_conv_mix': nrm(ks[5], (DEPTH, DEC_BATCH, CONV_W - 1, D_CONV), 1.0),
        'state_conv_ffn': nrm(ks[6], (DEPTH, DEC_BATCH, CONV_W - 1, D_FF), 1.0),
        'norm_mix': 1.0 + nrm(ks[7], (DEPTH, D_MODEL), 0.02),
        'w_in': nrm(ks[8], (DEPTH, D_MODEL, D_IN_PROJ), D_MODEL ** -0.5),
        'conv_mix_w': nrm(ks[9], (DEPTH, CONV_W, D_CONV), CONV_W ** -0.5),
        'w_conv_out': nrm(ks[10], (DEPTH, D_CONV, D_MODEL), D_CONV ** -0.5),
        'w_attn_out': nrm(ks[11], (DEPTH, ATT_W, D_MODEL), ATT_W ** -0.5),
        'w_out': nrm(ks[12], (DEPTH, D_MODEL, D_MODEL), D_MODEL ** -0.5),
        'norm_ffn': 1.0 + nrm(ks[13], (DEPTH, D_MODEL), 0.02),
        'w_ffn_in': nrm(ks[14], (DEPTH, D_MODEL, 2 * D_FF), D_MODEL ** -0.5),
        'ffn_conv_w': nrm(ks[15], (DEPTH, CONV_W, D_FF), CONV_W ** -0.5),
        'ffn_conv_b': nrm(ks[16], (DEPTH, D_FF), 0.01),
        'w_ffn_down': nrm(ks[17], (DEPTH, D_FF, D_MODEL), D_FF ** -0.5),
        'norm_final': 1.0 + nrm(ks[18], (D_MODEL,), 0.02),
    }

def reference(x_prompt, x_sample, cache_kv_g1, cache_kv_g2, cache_kv_g3, state_conv_mix, state_conv_ffn,
              norm_mix, w_in, conv_mix_w, w_conv_out, w_attn_out, w_out, norm_ffn, w_ffn_in,
              ffn_conv_w, ffn_conv_b, w_ffn_down, norm_final):
    b, t = x_prompt.shape[0], x_prompt.shape[1]
    pos_p = jnp.arange(t)
    pos_s = PAST_LEN + jnp.arange(x_sample.shape[1])
    caches = (cache_kv_g1, cache_kv_g2, cache_kv_g3)
    xp, xs = x_prompt, x_sample
    p_kv = [[] for _ in range(N_GROUPS)]
    s_kv = [[] for _ in range(N_GROUPS)]
    p_conv, p_ffn, s_conv, s_ffn = [], [], [], []
    for l in range(DEPTH):
        lw = (norm_mix[l], w_in[l], conv_mix_w[l], w_conv_out[l], w_attn_out[l], w_out[l],
              norm_ffn[l], w_ffn_in[l], ffn_conv_w[l], ffn_conv_b[l], w_ffn_down[l])
        zc = jnp.zeros((b, CONV_W - 1, D_CONV), xp.dtype)
        zf = jnp.zeros((b, CONV_W - 1, D_FF), xp.dtype)
        xp, pc, pf, pkv = decoder_layer(xp, pos_p, zc, zf, attend_prompt, *lw)
        attend_s = functools.partial(attend_sample, bufs=[c[l] for c in caches])
        xs, sc, sf, skv = decoder_layer(xs, pos_s, state_conv_mix[l], state_conv_ffn[l], attend_s, *lw)
        p_conv.append(pc)
        p_ffn.append(pf)
        s_conv.append(sc)
        s_ffn.append(sf)
        for g in range(N_GROUPS):
            p_kv[g].append(pkv[g])
            s_kv[g].append(skv[g])
    y_prompt = rmsnorm(xp, norm_final)
    y_sample = rmsnorm(xs, norm_final)
    return (y_prompt, y_sample,
            jnp.stack(p_kv[0]), jnp.stack(p_kv[1]), jnp.stack(p_kv[2]), jnp.stack(p_conv), jnp.stack(p_ffn),
            jnp.stack(s_kv[0]), jnp.stack(s_kv[1]), jnp.stack(s_kv[2]), jnp.stack(s_conv), jnp.stack(s_ffn))


_drawn_inputs = setup_inputs


def setup_inputs(seed=0):
    import zlib

    import numpy as np

    out = dict(_drawn_inputs(seed))
    spreads = {}
    factors = {'norm_ffn': 2.869, 'ffn_conv_b': 8.0, 'norm_final': 2.818}
    for name, (base, spread) in spreads.items():
        noise = np.random.default_rng([zlib.crc32(name.encode()), seed]).standard_normal(out[name].shape)
        drawn = base * np.exp(spread * noise) if base else spread * noise
        out[name] = __import__('jax').numpy.asarray(drawn.astype(out[name].dtype))
    for name, factor in factors.items():
        out[name] = (out[name] * factor).astype(out[name].dtype)
    return out
```

```python
from contextlib import ExitStack

import numpy as np

import concourse.bass as bass
from concourse import mybir

F32 = mybir.dt.float32
F32R = mybir.dt.float32r
ALU = mybir.AluOpType
ACT = mybir.ActivationFunctionType
AX_X = mybir.AxisListType.X

P = 128
D_MODEL = 2048
D_CONV = 1024
D_FF = 5632
HEADS = 4
HEAD_DIM = 128
GROUPS = ((128, 1), (512, 4), (2048, 16))
NG = len(GROUPS)
SUB_WIN = 128
ATT_W = HEADS * HEAD_DIM
SEQ = 256
BATCH = 8
PAST = 256
T = SEQ + BATCH
EPS = 1e-6
THETA = 10000.0
SCALE = HEAD_DIM ** -0.5

KT = D_MODEL // P
CT = D_CONV // P
FT = D_FF // P
GW = 512
RING = 4
AHEAD = 3
TILES = GW // P

N_MODEL, N_CONV, N_ATT = KT // 2, CT // 2, ATT_W // P // 2
PAIRS_A, PAIRS_B = 6, 5
N_DOWN_A, N_DOWN_B = PAIRS_A * TILES // 2, PAIRS_B * TILES // 2
PHASES = (("qkv", 9, N_MODEL), ("ucb", 6, N_MODEL), ("gate_a", 4, N_MODEL), ("conv_out", 4, N_CONV),
          ("gate_b", 4, N_MODEL), ("attn_out", 4, N_ATT), ("w_out", 4, N_MODEL),
          ("ffn_a", 2 * PAIRS_A, N_MODEL), ("down_a", 4, N_DOWN_A),
          ("ffn_b", 2 * PAIRS_B, N_MODEL), ("down_b", 4, N_DOWN_B))
GROUP0, QUAD0 = {}, {}
_g = _c = 0
for _name, _n, _chunks in PHASES:
    assert _c % RING == 0
    GROUP0[_name], QUAD0[_name] = _g, _c // RING
    _g, _c = _g + _n, _c + _n * _chunks
CHUNKS = _c

SAMPLE_ROWS = tuple(min(w, PAST) // d for w, d in GROUPS)
ROWS_A = SAMPLE_ROWS[0]
ROW_G2, ROW_OWN = SAMPLE_ROWS[1], SAMPLE_ROWS[1] + SAMPLE_ROWS[2]
ROWS_B = ROW_OWN + NG
SAMPLE_KEYS = ROWS_A + ROWS_B

PAR_G1, PAR_G2, PAR_GF = 0, KT, 2 * KT
PAR_CW = 3 * KT
PAR_FW = PAR_CW + 3 * CT
PAR_FB = PAR_FW + 3 * FT
PAR_N = PAR_FB + FT
MASK_N = NG * P + NG * 2 * P
ST = 2 + 2 * BATCH


def trunk_program(nc, x_fm, w_in, w_conv_out, w_attn_out, w_out, w_ffn_in, w_ffn_down, params, rope_tab,
                  masks, ident_in, st_mix_in, st_ffn_in, caches, q_new, kv_new,
                  y_out, p_kv, s_kv, conv_state_out, ffn_state_out):
    with ExitStack() as ctx:
        def sem(name):
            return ctx.enter_context(nc.semaphore(name))

        base = -(-nc.sbuf_base // 64) * 64
        size = {F32: 4, F32R: 4}
        cursor = [base]

        def place(name, shape, dt=F32, at=None):
            off = cursor[0] if at is None else at
            n = size[dt] * int(np.prod(shape[1:]))
            t = nc.alloc_sbuf_tensor_at(name, list(shape), dt, offset=off)
            if at is None:
                cursor[0] = off + -(-n // 32) * 32
            return t

        raw = place("raw", [P, RING, 2, GW])
        w_hi = place("w_hi", [P, RING, 2, GW], F32R)
        w_lo = place("w_lo", [P, RING, 2, GW], F32R)
        h_at = cursor[0]
        h_hi = place("h_hi", [P, KT, T], F32R)
        h_lo = place("h_lo", [P, KT, T], F32R)
        rot_at = cursor[0]
        rot = place("rot", [P, 2, T])
        rot_r = place("rot_r", [P, 2, T])
        r = place("r", [P, T])
        r2 = place("r2", [P, T])
        part = place("part", [P, 4, T])
        par = place("par", [P, PAR_N])
        ident = place("ident", [P, P])
        ones = place("ones", [P, P])
        st_mix = place("st_mix", [P, 2, CT, BATCH])
        st_ffn = place("st_ffn", [P, 2, FT, BATCH])
        base_mix = place("base_mix", [P, CT, BATCH])
        base_ffn = place("base_ffn", [P, FT, BATCH])
        tap_tmp = place("tap_tmp", [P, FT, BATCH])
        keep_mix = place("keep_mix", [P, CT, ST])
        keep_ffn = place("keep_ffn", [P, FT, ST])
        sc_a = place("sc_a", [ROWS_A, BATCH * HEADS])
        sc_b = place("sc_b", [ROWS_B, BATCH * HEADS])
        pt_a = place("pt_a", [ROWS_A, BATCH * HEADS])
        pt_b = place("pt_b", [ROWS_B, BATCH * HEADS])
        small = place("small", [P, 4, 2 * HEADS])
        ssmall = place("ssmall", [BATCH * HEADS, 4])
        sprob = place("sprob", [BATCH * HEADS, SAMPLE_KEYS])
        ab_at = cursor[0]
        ab_hi = place("ab_hi", [P, CT, T], F32R)
        ab_lo = place("ab_lo", [P, CT, T], F32R)
        x_in = place("x_in", [P, KT, T], at=ab_at)
        x = place("x", [P, KT, T], at=ab_at)
        att_hi = place("att_hi", [P, HEADS, T], F32R)
        att_lo = place("att_lo", [P, HEADS, T], F32R)
        zone = cursor[0]
        qkv = place("qkv", [P, 3 * NG * HEADS, T])
        sq0 = place("sq0", [P, KT, T], at=zone + 4 * 12 * T)
        vtok = place("vtok", [P, 2, NG * HEADS * HEAD_DIM])
        mask = place("mask", [P, MASK_N])
        tmp_at = cursor[0]
        qraw = place("qraw", [P, HEADS, T])
        qswap = place("qswap", [P, HEADS, T])
        prob = place("prob", [P, NG * 2 * P], at=tmp_at)
        prob_t = place("prob_t", [P, NG * 2 * P], at=tmp_at + 4 * NG * 2 * P)
        ub = place("ub", [P, TILES, T])
        zb = place("zb", [P, TILES, T + 2])
        yb = place("yb", [P, TILES, T])
        att_f = place("att_f", [P, P])
        sgath = place("sgath", [P, 3, NG * HEADS * BATCH])
        srow = place("srow", [NG * HEADS * BATCH, 3, HEAD_DIM])
        end_b = cursor[0]
        cursor[0] = zone
        gate_a = place("gate_a", [P, KT, T])
        gate_b = place("gate_b", [P, KT, T])
        mix_at = cursor[0]
        v_a = place("v_a", [ROWS_A, BATCH, ATT_W])
        v_b = place("v_b", [ROWS_B, BATCH, ATT_W])
        k_a = place("k_a", [ROWS_A, 2, ATT_W])
        k_b = place("k_b", [ROWS_B, 2, ATT_W])
        q_a = place("q_a", [ROWS_A, 2, ATT_W])
        q_b = place("q_b", [ROWS_B, 2, ATT_W], at=rot_at)
        end_c = cursor[0]
        cursor[0] = mix_at
        t_hi = place("t_hi", [P, KT, T], F32R)
        t_lo = place("t_lo", [P, KT, T], F32R)
        tf = place("tf", [P, TILES, T])
        sq = place("sq", [P, TILES, T])
        end_d = cursor[0]
        cursor[0] = zone
        f_hi = place("f_hi", [P, TILES * PAIRS_A, T], F32R)
        f_lo = place("f_lo", [P, TILES * PAIRS_A, T], F32R)
        fz = place("fz", [P, TILES, T + 2])
        fy = place("fy", [P, TILES, T])
        ff = place("ff", [P, TILES, T])
        fsq = place("fsq", [P, TILES, T])
        yg = place("yg", [P, KT, T], at=h_at)
        end_e = cursor[0]
        assert max(end_b, end_c, end_d, end_e) <= nc.sbuf_usable_end, (end_b, end_c, end_d, end_e, nc.sbuf_usable_end)

        acc = ctx.enter_context(nc.psum_tensor("acc", [P, TILES, 512], F32))
        side = ctx.enter_context(nc.psum_tensor("side", [P, 4 * 512], F32))
        SCORES, TURNED, HEAD_OUT = 0, 2 * 512, 3 * 512 + 256
        STATS = 3 * 512

        holds = sem("holds")
        raw_landed = [sem(f"raw_landed{i}") for i in range(RING)]
        hi_ready, lo_ready = sem("hi_ready"), sem("lo_ready")
        slots_free = sem("slots_free")
        tile_done = sem("tile_done")
        psum_free = sem("psum_free")
        x_landed = [sem(f"x_landed{i}") for i in range(4)]
        par_landed, rot_landed, mask_landed, ident_landed, st_landed = (
            sem("par_landed"), sem("rot_landed"), sem("mask_landed"), sem("ident_landed"), sem("st_landed"))
        h_hi_ready, h_lo_ready, squared, part_ready = sem("h_hi_ready"), sem("h_lo_ready"), sem("squared"), sem("part_ready")
        sumsq_ready, ms_ready, r2_ready, r_ready = sem("sumsq_ready"), sem("ms_ready"), sem("r2_ready"), sem("r_ready")
        ones_ready, zpad_ready = sem("ones_ready"), sem("zpad_ready")
        rot_r_ready, swapped, rope_parts, roped = sem("rot_r_ready"), sem("swapped"), sem("rope_parts"), sem("roped")
        vt_done, vtok_ready = sem("vt_done"), sem("vtok_ready")
        scores_done, masked, negmax_ready, exp_ready, rsum_ready, prob_ready = (
            sem("scores_done"), sem("masked"), sem("negmax_ready"), sem("exp_ready"), sem("rsum_ready"), sem("prob_ready"))
        turned, prob_t_ready, head_done, att_f_ready, att_hi_ready, att_ready = (
            sem("turned"), sem("prob_t_ready"), sem("head_done"), sem("att_f_ready"), sem("att_hi_ready"), sem("att_ready"))
        tap2, tap1, conv_y, conv_yr, ab_hi_ready, ab_ready, z_kept = (
            sem("tap2"), sem("tap1"), sem("conv_y"), sem("conv_yr"), sem("ab_hi_ready"), sem("ab_ready"), sem("z_kept"))
        base_step, base_ready = sem("base_step"), sem("base_ready")
        gathered, srow_done, srow_ready, rows_sent, own_out = (
            sem("gathered"), sem("srow_done"), sem("srow_ready"), sem("rows_sent"), sem("own_out"))
        v_landed, kq_landed, prod_ready, scored = sem("v_landed"), sem("kq_landed"), sem("prod_ready"), sem("scored")
        sturned, snegated, smax_ready, sexp_ready, srsum_ready, sprob_ready, spt_done, spt_ready, shead_done = (
            sem("sturned"), sem("snegated"), sem("smax_ready"), sem("sexp_ready"), sem("srsum_ready"),
            sem("sprob_ready"), sem("spt_done"), sem("spt_ready"), sem("shead_done"))
        satt_f, satt_hi, satt_ready = sem("satt_f"), sem("satt_hi"), sem("satt_ready")
        gate_a_ready, gate_b_ready = sem("gate_a_ready"), sem("gate_b_ready")
        mixed, t_hi_ready, t_ready, x_back = sem("mixed"), sem("t_hi_ready"), sem("t_ready"), sem("x_back")
        fz_kept, ftap2, ftap1, fconv, fsilu, fscaled, f_hi_ready, f_ready = (
            sem("fz_kept"), sem("ftap2"), sem("ftap1"), sem("fconv"), sem("fsilu"), sem("fscaled"),
            sem("f_hi_ready"), sem("f_ready"))
        yg_ready, y_ready = sem("yg_ready"), sem("y_ready")
        kv_stored, cache_copied, state_stored, y_stored = sem("kv_stored"), sem("cache_copied"), sem("state_stored"), sem("y_stored")

        def wait_tile(eng, group, quad, n, m):
            if m < TILES - 1:
                eng.wait_ge(tile_done, (TILES - 1) * group + m + 1)
            else:
                eng.wait_ge(slots_free, 4 * quad + RING + n)

        def wait_taken(eng, group, m):
            eng.wait_ge(psum_free, TILES * group + TILES + m + 1)

        def held(eng):
            eng.sem_inc(holds, 1)

        def tiles(t, first, n=1):
            return t[:, bass.ds(first, n), :]

        def over_tiles(row, n=TILES):
            return row.unsqueeze(1).to_broadcast([P, n, T])

        def par_col(col):
            return par[:, bass.ds(col, 1)]

        block = ctx.enter_context(nc.Block())

        @block.sync
        def _(sp):
            def load(weights, k0, col, quad, s, wait=True):
                if wait:
                    sp.wait_ge(lo_ready, 4 * quad + s - RING + 1)
                    held(sp)
                src = weights[k0 * P:(k0 + 2) * P, bass.ds(col, GW)].rearrange("(k p) n -> p k n", p=P)
                sp.dma_start(raw[:, s % RING], src).then_inc(raw_landed[s % RING], 16)

            def group(weights, n, col, quad, s0=0, k0=0):
                for s in range(n):
                    load(weights, k0 + 2 * s, col, quad, s0 + s)

            qkv_col = 3 * D_CONV
            for s in range(N_MODEL):
                load(w_in, 2 * s, qkv_col, 0, s, wait=s >= RING)
            with sp.Fori(1, 9) as i:
                group(w_in, N_MODEL, GW * i + qkv_col, 2 * i)
            for i in range(6):
                col = (0, 2 * D_CONV, D_CONV)[i % 3] + GW * (i // 3)
                group(w_in, N_MODEL, col, QUAD0["ucb"] + 2 * i)
            gate_col = 3 * D_CONV + 9 * ATT_W
            with sp.Fori(0, 4) as i:
                group(w_in, N_MODEL, GW * i + gate_col, 2 * i + QUAD0["gate_a"])
            with sp.Fori(0, 4) as i:
                group(w_conv_out, N_CONV, GW * i, i + QUAD0["conv_out"])
            with sp.Fori(0, 4) as i:
                group(w_in, N_MODEL, GW * i + (gate_col + D_MODEL), 2 * i + QUAD0["gate_b"])
            with sp.Fori(0, 2) as i:
                group(w_attn_out, N_ATT, 2 * GW * i, i + QUAD0["attn_out"])
                group(w_attn_out, N_ATT, 2 * GW * i + GW, i + QUAD0["attn_out"], s0=N_ATT)
            with sp.Fori(0, 4) as i:
                group(w_out, N_MODEL, GW * i, 2 * i + QUAD0["w_out"])
            for half, pairs, n, first in (("a", PAIRS_A, N_DOWN_A, 0), ("b", PAIRS_B, N_DOWN_B, PAIRS_A)):
                with sp.Fori(0, pairs) as i:
                    group(w_ffn_in, N_MODEL, GW * i + (D_FF + GW * first), 4 * i + QUAD0["ffn_" + half])
                    group(w_ffn_in, N_MODEL, GW * i + GW * first, 4 * i + QUAD0["ffn_" + half], s0=N_MODEL)
                with sp.Fori(0, 2) as i:
                    quad = (2 * n // RING) * i + QUAD0["down_" + half]
                    group(w_ffn_down, n, 2 * GW * i, quad, k0=TILES * first)
                    group(w_ffn_down, n, 2 * GW * i + GW, quad, s0=n, k0=TILES * first)
            for q in range(4):
                sp.wait_ge(y_ready, q + 1)
                sp.dma_start(y_out[:, 4 * q:4 * q + 4, :], yg[:, 4 * q:4 * q + 4, :]).then_inc(y_stored, 16)
            sp.wait_ge(y_stored, 64)
            sp.wait_ge(kv_stored, 16 * NG)
            sp.wait_ge(own_out, 16 * NG)
            sp.wait_ge(cache_copied, 16 * NG * BATCH)
            sp.wait_ge(state_stored, 32)

        @block.scalar
        def _(act):
            def hi(quad, s):
                act.wait_ge(raw_landed[s % RING], 16 * quad + 16 * (s // RING + 1))
                act.wait_ge(slots_free, 4 * quad + s + 1)
                act.activation(w_hi[:, s % RING], raw[:, s % RING], ACT.Copy).then_inc(hi_ready, 1)

            def his(quad, s0, s1):
                for s in range(s0 + AHEAD, s1 + AHEAD):
                    hi(quad, s)

            def split_rows(norm, src, first, par0):
                for m in range(TILES):
                    if norm:
                        wait_taken(act, first["group"], m)
                        held(act)
                    act.activation(tiles(h_hi, first["tile"] + m), tiles(src, first["tile"] + m), ACT.Copy,
                                   scale=par_col(first["tile"] + (par0 + m))).then_inc(h_hi_ready, 1)

            def inverse_root(norm):
                act.wait_ge(r2_ready, norm + 1)
                act.activation(r[:, :], r2[:, :], ACT.Sqrt).then_inc(r_ready, 1)

            act.wait_ge(par_landed, 16)
            for q in range(4):
                act.wait_ge(x_landed[q], 16)
                split_rows(0, x_in, {"tile": 4 * q}, PAR_G1)
                act.activation(sq0[:, 4 * q:4 * q + 4, :], x_in[:, 4 * q:4 * q + 4, :], ACT.Square).then_inc(squared, 1)
                if q < AHEAD:
                    hi(0, q)

            def rope_inputs(group, unit, wait):
                for m in range(TILES):
                    wait_tile(act, group, 2 * group, N_MODEL, m)
                    if m == 0 and wait:
                        act.wait_ge(roped, unit)
                    act.activation(qraw[:, m, :], acc[:, m, 0:T], ACT.Copy).then_inc(psum_free, 1)
                wait_taken(act, group, TILES - 1)
                for dst, src in ((0, 64), (64, 0)):
                    act.activation(qswap[dst:dst + 64, :, :], qraw[src:src + 64, :, :], ACT.Copy).then_inc(swapped, 1)

            def qkv_body(g, peeled):
                his(6 * g, 0, N_MODEL)
                if peeled:
                    inverse_root(0)
                rope_inputs(3 * g, 2 * g, not peeled)
                his(6 * g, N_MODEL, 2 * N_MODEL)
                rope_inputs(3 * g + 1, 2 * g + 1, True)
                his(6 * g, 2 * N_MODEL, 3 * N_MODEL)

            qkv_body(0, True)
            with act.Fori(1, NG) as g:
                qkv_body(g, False)

            def exp_unit(u):
                h, qt = u // 2, u % 2
                n = NG * P * (qt + 1)
                act.wait_ge(negmax_ready, u + 1)
                act.activation(prob[:, 0:n], prob[:, 0:n], ACT.Exp, bias=small[:, 0, u:u + 1], scale=-1.0,
                               accum_out=small[:, 1, u:u + 1]).then_inc(exp_ready, 1)

            def probs_out(u):
                n = NG * P * (u % 2 + 1)
                act.wait_ge(turned, u + 1)
                act.activation(prob_t[:, 0:n], side[:, TURNED:TURNED + n], ACT.Copy).then_inc(prob_t_ready, 1)

            for slot in range(6 * N_MODEL):
                hi(QUAD0["ucb"], slot + AHEAD)
                if slot < NG:
                    for qt in range(2):
                        act.wait_ge(vt_done, 2 * slot + qt + 1)
                        bank = 2 * (slot % 2) + qt
                        act.activation(vtok[:, qt, slot * ATT_W:(slot + 1) * ATT_W],
                                       side[:, 512 * bank:512 * (bank + 1)], ACT.Copy).then_inc(vtok_ready, 1)
                if slot == NG:
                    act.wait_ge(srow_done, 1)
                    act.activation(srow[:, :, :].rearrange("p a d -> p (a d)"),
                                   side[0:NG * HEADS * BATCH, 1024:1024 + 3 * HEAD_DIM], ACT.Copy).then_inc(srow_ready, 1)
                for j in range(2):
                    if slot == 24 * j + 17:
                        for m in range(TILES):
                            wait_taken(act, GROUP0["ucb"] + 3 * j + 1, m)
                            act.activation(yb[:, m, :], zb[:, m, 2:2 + T], ACT.Copy,
                                           scale=par_col(PAR_CW + 2 * CT + 4 * j + m)).then_inc(tap2, 1)
                    if slot == 24 * j + 23:
                        wait_taken(act, GROUP0["ucb"] + 3 * j + 2, TILES - 1)
                        act.activation(ab_hi[:, 4 * j:4 * j + 4, :], ub[:, :, :], ACT.Copy).then_inc(ab_hi_ready, 1)
                for u in range(2 * HEADS):
                    if slot == 5 * u + 5:
                        exp_unit(u)
                    if slot == 5 * u + 7:
                        probs_out(u)

            def gates(name, out, ready):
                with act.Fori(0, 4) as i:
                    his(2 * i + QUAD0[name], 0, N_MODEL)
                    wait_taken(act, i + GROUP0[name], TILES - 1)
                    held(act)
                    act.activation(tiles(out, 4 * i, 4), tiles(out, 4 * i, 4), ACT.Sigmoid).then_inc(ready, 1)

            gates("gate_a", gate_a, gate_a_ready)
            act.wait_ge(smax_ready, 1)
            act.activation(sprob[:, :], sprob[:, :], ACT.Exp, bias=ssmall[:, 0:1], scale=-1.0,
                           accum_out=ssmall[:, 1:2]).then_inc(sexp_ready, 1)
            with act.Fori(0, 4) as i:
                his(i + QUAD0["conv_out"], 0, N_CONV)
            act.wait_ge(spt_done, 2)
            act.activation(pt_a[:, :], side[0:ROWS_A, 512:512 + BATCH * HEADS], ACT.Copy).then_inc(spt_ready, 1)
            act.activation(pt_b[:, :], side[0:ROWS_B, 544:544 + BATCH * HEADS], ACT.Copy).then_inc(spt_ready, 1)
            gates("gate_b", gate_b, gate_b_ready)
            with act.Fori(0, 2) as i:
                for half in range(2):
                    his(i + QUAD0["attn_out"], N_ATT * half, N_ATT * (half + 1))
                    act.wait_ge(mixed, 2 * i + half + 1)
                    held(act)
                    act.activation(tiles(t_hi, 8 * i + 4 * half, 4), tf[:, :, :], ACT.Copy).then_inc(t_hi_ready, 1)
            with act.Fori(0, 4) as i:
                his(2 * i + QUAD0["w_out"], 0, N_MODEL)
                split_rows(1, x, {"tile": 4 * i, "group": i + GROUP0["w_out"]}, PAR_G2)
                act.wait_ge(part_ready, i + 4)
                held(act)
                act.activation(sq[:, :, :], tiles(x, 4 * i, 4), ACT.Square).then_inc(squared, 1)

            def ffn_pair(half, pair0, i, peeled):
                quad, g = 4 * i + QUAD0["ffn_" + half], 2 * i + GROUP0["ffn_" + half]
                p = i + pair0
                his(quad, 0, 7)
                if peeled:
                    inverse_root(1)
                his(quad, 7, N_MODEL)
                for m in range(TILES):
                    wait_taken(act, g, m)
                    held(act)
                    act.activation(fy[:, m, :], fz[:, m, 2:2 + T], ACT.Identity, bias=par_col(4 * p + (PAR_FB + m)),
                                   scale=par_col(4 * p + (PAR_FW + 2 * FT + m))).then_inc(ftap2, 1)
                his(quad, N_MODEL, N_MODEL + 4)
                act.wait_ge(fconv, 5 * p + 5)
                act.activation(fy[:, :, :], fy[:, :, :], ACT.Silu).then_inc(fsilu, 1)
                his(quad, N_MODEL + 4, 2 * N_MODEL)
                wait_taken(act, g + 1, TILES - 1)
                held(act)
                act.activation(tiles(f_hi, 4 * i, 4), ff[:, :, :], ACT.Copy).then_inc(f_hi_ready, 1)

            ffn_pair("a", 0, 0, True)
            with act.Fori(1, PAIRS_A) as i:
                ffn_pair("a", 0, i, False)
            with act.Fori(0, 2) as i:
                his((2 * N_DOWN_A // RING) * i + QUAD0["down_a"], 0, 2 * N_DOWN_A)
            with act.Fori(0, PAIRS_B) as i:
                ffn_pair("b", PAIRS_A, i, False)
            for j in range(4):
                quad = QUAD0["down_b"] + (2 * N_DOWN_B // RING) * (j // 2)
                s0 = N_DOWN_B * (j % 2)
                his(quad, s0, s0 + N_DOWN_B - (AHEAD if j == 3 else 0))
                act.wait_ge(part_ready, 8 + j)
                wait_taken(act, GROUP0["down_b"] + j, TILES - 1)
                act.activation(fsq[:, :, :], x[:, 4 * j:4 * j + 4, :], ACT.Square).then_inc(squared, 1)
                for m in range(TILES):
                    act.activation(yg[:, 4 * j + m, :], x[:, 4 * j + m, :], ACT.Copy,
                                   scale=par_col(PAR_GF + 4 * j + m)).then_inc(yg_ready, 1)
            inverse_root(2)

        @block.vector
        def _(dve):
            def lo(quad, s):
                dve.wait_ge(hi_ready, 4 * quad + s + 1)
                dve.tensor_tensor(w_lo[:, s % RING], raw[:, s % RING], w_hi[:, s % RING].bitcast(F32),
                                  ALU.subtract).then_inc(lo_ready, 1)

            def los(quad, s0, s1):
                for s in range(s0 + AHEAD, s1 + AHEAD):
                    lo(quad, s)

            def split_rows(src, tile, ready0, par0):
                for m in range(TILES):
                    dve.wait_ge(h_hi_ready, tile + (ready0 + m + 1))
                    dve.scalar_tensor_tensor(tiles(h_lo, tile + m), tiles(src, tile + m), par_col(tile + (par0 + m)),
                                             tiles(h_hi, tile + m).bitcast(F32), ALU.mult,
                                             ALU.subtract).then_inc(h_lo_ready, 1)

            def sum_squares(squares, norm, q):
                dve.wait_ge(squared, q + (4 * norm + 1))
                dve.tensor_reduce(part[:, bass.ds(q, 1), :].rearrange("p a t -> p (a t)"), squares.rearrange("p m t -> p t m"),
                                  AX_X, ALU.add).then_inc(part_ready, 1)

            def row_factor(norm):
                dve.wait_ge(sumsq_ready, norm + 1)
                dve.tensor_scalar(r2[:, :], side[:, STATS:STATS + T], 1.0 / D_MODEL, EPS, ALU.mult,
                                  ALU.add).then_inc(ms_ready, 1)
                dve.wait_ge(ms_ready, norm + 1)
                dve.reciprocal(r2[:, :], r2[:, :]).then_inc(r2_ready, 1)

            dve.wait_ge(par_landed, 16)
            for q in range(4):
                split_rows(x_in, 4 * q, 0, PAR_G1)
                if q < AHEAD:
                    lo(0, q)
            for q in range(4):
                sum_squares(sq0[:, 4 * q:4 * q + 4, :], 0, q)

            def rope(unit, first):
                out = tiles(qkv, first, 4)
                dve.wait_ge(swapped, 2 * unit + 2)
                dve.tensor_tensor(out, qraw[:, :, :], over_tiles(rot_r[:, 0, :]), ALU.mult).then_inc(rope_parts, 1)
                dve.tensor_tensor(qswap[:, :, :], qswap[:, :, :], over_tiles(rot_r[:, 1, :]), ALU.mult).then_inc(rope_parts, 1)
                dve.wait_ge(rope_parts, 2 * unit + 2)
                dve.tensor_tensor(out, out, qswap[:, :, :], ALU.add).then_inc(roped, 1)

            def qkv_body(g, peeled):
                quad = 6 * g
                if peeled:
                    los(quad, 0, N_MODEL - 1)
                    row_factor(0)
                    los(quad, N_MODEL - 1, N_MODEL)
                    dve.wait_ge(r_ready, 1)
                    dve.wait_ge(rot_landed, 16)
                    dve.tensor_tensor(rot_r[:, :, :], rot[:, :, :], over_tiles(r[:, :], 2), ALU.mult).then_inc(rot_r_ready, 1)
                    dve.wait_ge(rot_r_ready, 1)
                else:
                    los(quad, 0, N_MODEL)
                los(quad, N_MODEL, N_MODEL + 4)
                rope(2 * g, 12 * g)
                los(quad, N_MODEL + 4, 2 * N_MODEL + 4)
                rope(2 * g + 1, 12 * g + 4)
                los(quad, 2 * N_MODEL + 4, 3 * N_MODEL)
                for m in range(TILES):
                    wait_tile(dve, 3 * g + 2, quad, 3 * N_MODEL, m)
                    dve.tensor_tensor(tiles(qkv, 12 * g + 8 + m), acc[:, m:m + 1, 0:T], over_tiles(r[:, :], 1),
                                      ALU.mult).then_inc(psum_free, 1)

            qkv_body(0, True)
            with dve.Fori(1, NG) as g:
                qkv_body(g, False)

            dve.wait_ge(mask_landed, 16)
            for slot in range(6 * N_MODEL):
                lo(QUAD0["ucb"], slot + AHEAD)
                group, j = GROUP0["ucb"] + slot // N_MODEL, slot // 24
                for u in range(2 * HEADS):
                    h, qt = u // 2, u % 2
                    n = NG * P * (qt + 1)
                    if slot == 5 * u + 4:
                        dve.wait_ge(scores_done, u + 1)
                        m0 = NG * P * qt
                        if u >= 1:
                            dve.wait_ge(turned, u)
                        dve.scalar_tensor_tensor(prob[:, 0:n], side[:, SCORES:SCORES + n], -SCALE, mask[:, m0:m0 + n],
                                                 ALU.mult, ALU.add).then_inc(masked, 1)
                        dve.wait_ge(masked, u + 1)
                        dve.tensor_reduce(small[:, 0, u:u + 1], prob[:, 0:n], AX_X, ALU.min).then_inc(negmax_ready, 1)
                    if slot == 5 * u + 6:
                        dve.wait_ge(exp_ready, u + 1)
                        dve.reciprocal(small[:, 2, u:u + 1], small[:, 1, u:u + 1]).then_inc(rsum_ready, 1)
                        dve.wait_ge(rsum_ready, u + 1)
                        dve.tensor_scalar(prob[:, 0:n], prob[:, 0:n], small[:, 2, u:u + 1], None,
                                          ALU.mult).then_inc(prob_ready, 1)
                    if slot == 5 * u + 8:
                        cols = slice(qt * P, (qt + 1) * P)
                        dve.wait_ge(head_done, u + 1)
                        dve.tensor_copy(att_f[:, :], side[:, HEAD_OUT:HEAD_OUT + P]).then_inc(att_f_ready, 1)
                        dve.wait_ge(att_f_ready, u + 1)
                        dve.tensor_copy(att_hi[:, h, cols], att_f[:, :]).then_inc(att_hi_ready, 1)
                        dve.wait_ge(att_hi_ready, u + 1)
                        dve.tensor_tensor(att_lo[:, h, cols], att_f[:, :], att_hi[:, h, cols].bitcast(F32),
                                          ALU.subtract).then_inc(att_ready, 1)
                if slot == 24 * j + 7:
                    for m in range(TILES):
                        wait_tile(dve, group, 2 * group, N_MODEL, m)
                        dve.tensor_tensor(ub[:, m, :], acc[:, m, 0:T], r2[:, :], ALU.mult).then_inc(psum_free, 1)
                if slot == 24 * j + 15:
                    dve.wait_ge(zpad_ready, 1)
                    if j:
                        dve.wait_ge(z_kept, 2)
                    wait_taken(dve, group - 1, TILES - 1)
                    for m in range(TILES):
                        wait_tile(dve, group, 2 * group, N_MODEL, m)
                        dve.tensor_tensor(zb[:, m, 2:2 + T], acc[:, m, 0:T], ub[:, m, :], ALU.mult).then_inc(psum_free, 1)
                if slot == 24 * j + 18:
                    for m in range(TILES):
                        dve.wait_ge(tap2, 4 * j + m + 1)
                        dve.scalar_tensor_tensor(yb[:, m, 0:SEQ], zb[:, m, 1:1 + SEQ], par_col(PAR_CW + CT + 4 * j + m),
                                                 yb[:, m, 0:SEQ], ALU.mult, ALU.add).then_inc(tap1, 1)
                if slot == 24 * j + 19:
                    for m in range(TILES):
                        dve.wait_ge(tap1, 4 * j + m + 1)
                        dve.scalar_tensor_tensor(yb[:, m, 0:SEQ], zb[:, m, 0:SEQ], par_col(PAR_CW + 4 * j + m),
                                                 yb[:, m, 0:SEQ], ALU.mult, ALU.add).then_inc(conv_y, 1)
                    dve.wait_ge(base_ready, 1)
                    dve.tensor_tensor(yb[:, :, SEQ:T], yb[:, :, SEQ:T], base_mix[:, 4 * j:4 * j + 4, :],
                                      ALU.add).then_inc(conv_y, 1)
                if slot == 24 * j + 20:
                    dve.wait_ge(conv_y, 5 * j + 5)
                    dve.tensor_tensor(yb[:, :, :], yb[:, :, :], over_tiles(r[:, :]), ALU.mult).then_inc(conv_yr, 1)
                if slot == 24 * j + 23:
                    dve.wait_ge(conv_yr, j + 1)
                    for m in range(TILES):
                        wait_tile(dve, group, 2 * group, N_MODEL, m)
                        dve.tensor_tensor(ub[:, m, :], acc[:, m, 0:T], yb[:, m, :], ALU.mult).then_inc(psum_free, 1)
                    dve.wait_ge(ab_hi_ready, j + 1)
                    dve.tensor_tensor(ab_lo[:, 4 * j:4 * j + 4, :], ub[:, :, :], ab_hi[:, 4 * j:4 * j + 4, :].bitcast(F32),
                                      ALU.subtract).then_inc(ab_ready, 1)

            def take_gate(name, i, out):
                for m in range(TILES):
                    wait_tile(dve, i + GROUP0[name], 2 * i + QUAD0[name], N_MODEL, m)
                    dve.tensor_tensor(tiles(out, 4 * i + m), acc[:, m:m + 1, 0:T], over_tiles(r[:, :], 1),
                                      ALU.mult).then_inc(psum_free, 1)

            dve.wait_ge(kv_stored, 16 * NG)
            dve.wait_ge(rows_sent, 16 * 3 * NG)
            with dve.Fori(0, 4) as i:
                los(2 * i + QUAD0["gate_a"], 0, 5)
                dve.wait_ge(kq_landed, 128 * i + 128)
                dve.tensor_tensor(k_a[:, :, :], k_a[:, :, :], q_a[:, :, :], ALU.mult).then_inc(prod_ready, 1)
                dve.tensor_tensor(k_b[:, :, :], k_b[:, :, :], q_b[:, :, :], ALU.mult).then_inc(prod_ready, 1)
                los(2 * i + QUAD0["gate_a"], 5, 6)
                dve.wait_ge(prod_ready, 2 * i + 2)
                for out, prod in ((sc_a, k_a), (sc_b, k_b)):
                    dve.tensor_reduce(out[:, bass.ds(2 * HEADS * i, 2 * HEADS)],
                                      prod[:, :, :].rearrange("p b (h d) -> p (b h) d", h=HEADS),
                                      AX_X, ALU.add).then_inc(scored, 1)
                los(2 * i + QUAD0["gate_a"], 6, N_MODEL)
                take_gate("gate_a", i, gate_a)
            dve.wait_ge(sturned, 2)
            dve.tensor_scalar(sprob[:, :], side[0:BATCH * HEADS, 0:SAMPLE_KEYS], -SCALE, None, ALU.mult).then_inc(snegated, 1)
            dve.wait_ge(snegated, 1)
            dve.tensor_reduce(ssmall[:, 0:1], sprob[:, :], AX_X, ALU.min).then_inc(smax_ready, 1)
            dve.wait_ge(sexp_ready, 1)
            dve.reciprocal(ssmall[:, 2:3], ssmall[:, 1:2]).then_inc(srsum_ready, 1)
            dve.wait_ge(srsum_ready, 1)
            dve.tensor_scalar(sprob[:, :], sprob[:, :], ssmall[:, 2:3], None, ALU.mult).then_inc(sprob_ready, 1)
            with dve.Fori(0, 4) as i:
                los(i + QUAD0["conv_out"], 0, N_CONV)
                dve.wait_ge(gate_a_ready, 4)
                for m in range(TILES):
                    wait_tile(dve, i + GROUP0["conv_out"], i + QUAD0["conv_out"], N_CONV, m)
                    dve.tensor_tensor(tiles(gate_a, 4 * i + m), acc[:, m:m + 1, 0:T], tiles(gate_a, 4 * i + m),
                                      ALU.mult).then_inc(psum_free, 1)
            with dve.Fori(0, 4) as i:
                los(2 * i + QUAD0["gate_b"], 0, N_MODEL)
                take_gate("gate_b", i, gate_b)
            dve.wait_ge(shead_done, 1)
            sout = side[:, 1024:1024 + HEADS * BATCH].rearrange("p (h b) -> p h b", h=HEADS)
            satt = tf[:, :, SEQ:T]
            dve.tensor_copy(satt, sout).then_inc(satt_f, 1)
            dve.wait_ge(satt_f, 1)
            dve.tensor_copy(att_hi[:, :, SEQ:T], satt).then_inc(satt_hi, 1)
            dve.wait_ge(satt_hi, 1)
            dve.tensor_tensor(att_lo[:, :, SEQ:T], satt, att_hi[:, :, SEQ:T].bitcast(F32), ALU.subtract).then_inc(satt_ready, 1)
            dve.wait_ge(gate_b_ready, 4)
            with dve.Fori(0, 2) as i:
                for half in range(2):
                    los(i + QUAD0["attn_out"], N_ATT * half, N_ATT * (half + 1))
                    g, first = 2 * i + (half + GROUP0["attn_out"]), 8 * i + 4 * half
                    for m in range(TILES):
                        wait_tile(dve, g, i + QUAD0["attn_out"], N_ATT * (half + 1), m)
                        dve.tensor_tensor(tf[:, m:m + 1, :], acc[:, m:m + 1, 0:T], tiles(gate_b, first + m),
                                          ALU.mult).then_inc(psum_free, 1)
                    wait_taken(dve, g, TILES - 1)
                    dve.tensor_tensor(tf[:, :, :], tf[:, :, :], tiles(gate_a, first, 4), ALU.add).then_inc(mixed, 1)
                    dve.wait_ge(t_hi_ready, 2 * i + half + 1)
                    dve.tensor_tensor(tiles(t_lo, first, 4), tf[:, :, :], tiles(t_hi, first, 4).bitcast(F32),
                                      ALU.subtract).then_inc(t_ready, 1)
                    dve.wait_ge(t_ready, 2 * i + half + 1)

            def add_to_x(tile, group, quad, n):
                for m in range(TILES):
                    wait_tile(dve, group, quad, n, m)
                    dve.tensor_tensor(tiles(x, tile + m), acc[:, m:m + 1, 0:T], tiles(x, tile + m),
                                      ALU.add).then_inc(psum_free, 1)

            dve.wait_ge(x_back, 16)
            with dve.Fori(0, 4) as i:
                los(2 * i + QUAD0["w_out"], 0, N_MODEL)
                add_to_x(4 * i, i + GROUP0["w_out"], 2 * i + QUAD0["w_out"], N_MODEL)
                split_rows(x, 4 * i, KT, PAR_G2)
                sum_squares(sq[:, :, :], 1, i)

            def ffn_pair(half, pair0, i, peeled):
                quad, g = 4 * i + QUAD0["ffn_" + half], 2 * i + GROUP0["ffn_" + half]
                p = i + pair0
                los(quad, 0, 6)
                if peeled:
                    row_factor(1)
                los(quad, 6, N_MODEL)
                if peeled:
                    dve.wait_ge(r_ready, 2)
                else:
                    dve.wait_ge(fz_kept, 2 * p)
                for m in range(TILES):
                    wait_tile(dve, g, quad, N_MODEL, m)
                    dve.tensor_tensor(fz[:, m, 2:2 + T], acc[:, m, 0:T], r[:, :], ALU.mult).then_inc(psum_free, 1)
                los(quad, N_MODEL, N_MODEL + 2)
                for m in range(TILES):
                    dve.wait_ge(ftap2, 4 * p + m + 1)
                    dve.scalar_tensor_tensor(fy[:, m, 0:SEQ], fz[:, m, 1:1 + SEQ], par_col(4 * p + (PAR_FW + FT + m)),
                                             fy[:, m, 0:SEQ], ALU.mult, ALU.add).then_inc(ftap1, 1)
                los(quad, N_MODEL + 2, N_MODEL + 3)
                for m in range(TILES):
                    dve.wait_ge(ftap1, 4 * p + m + 1)
                    dve.scalar_tensor_tensor(fy[:, m, 0:SEQ], fz[:, m, 0:SEQ], par_col(4 * p + (PAR_FW + m)),
                                             fy[:, m, 0:SEQ], ALU.mult, ALU.add).then_inc(fconv, 1)
                dve.tensor_tensor(fy[:, :, SEQ:T], fy[:, :, SEQ:T], tiles(base_ffn, 4 * p, 4), ALU.add).then_inc(fconv, 1)
                los(quad, N_MODEL + 3, N_MODEL + 5)
                dve.wait_ge(fsilu, p + 1)
                dve.tensor_tensor(fy[:, :, :], fy[:, :, :], over_tiles(r[:, :]), ALU.mult).then_inc(fscaled, 1)
                los(quad, N_MODEL + 5, 2 * N_MODEL)
                dve.wait_ge(fscaled, p + 1)
                for m in range(TILES):
                    wait_tile(dve, g + 1, quad, 2 * N_MODEL, m)
                    dve.tensor_tensor(ff[:, m, :], acc[:, m, 0:T], fy[:, m, :], ALU.mult).then_inc(psum_free, 1)
                dve.wait_ge(f_hi_ready, p + 1)
                dve.tensor_tensor(tiles(f_lo, 4 * i, 4), ff[:, :, :], tiles(f_hi, 4 * i, 4).bitcast(F32),
                                  ALU.subtract).then_inc(f_ready, 1)

            dve.memset(fz[:, :, 0:2], 0.0).then_inc(zpad_ready, 1)
            dve.wait_ge(base_ready, 2)
            dve.wait_ge(zpad_ready, 2)
            ffn_pair("a", 0, 0, True)
            with dve.Fori(1, PAIRS_A) as i:
                ffn_pair("a", 0, i, False)
            with dve.Fori(0, 2) as i:
                quad = (2 * N_DOWN_A // RING) * i + QUAD0["down_a"]
                for half in range(2):
                    los(quad, N_DOWN_A * half, N_DOWN_A * (half + 1))
                    add_to_x(8 * i + 4 * half, 2 * i + (half + GROUP0["down_a"]), quad, N_DOWN_A * (half + 1))
            with dve.Fori(0, PAIRS_B) as i:
                ffn_pair("b", PAIRS_A, i, False)
            for j in range(4):
                quad = QUAD0["down_b"] + (2 * N_DOWN_B // RING) * (j // 2)
                s0 = N_DOWN_B * (j % 2)
                los(quad, s0, s0 + N_DOWN_B - (AHEAD if j == 3 else 0))
                add_to_x(4 * j, GROUP0["down_b"] + j, quad, s0 + N_DOWN_B)
                sum_squares(fsq[:, :, :], 2, j)
            row_factor(2)
            dve.wait_ge(r_ready, 3)
            for q in range(4):
                dve.wait_ge(yg_ready, 4 * q + 4)
                dve.tensor_tensor(yg[:, 4 * q:4 * q + 4, :], yg[:, 4 * q:4 * q + 4, :], over_tiles(r[:, :]),
                                  ALU.mult).then_inc(y_ready, 1)

        @block.tensor
        def _(pe):
            pe.sem_inc(slots_free, RING)
            pe.sem_inc(psum_free, TILES)

            def chunk(quad, s, group, first, last, m_hi, m_lo, kt):
                pe.wait_ge(lo_ready, 4 * quad + s + 1)
                slot = s % RING
                for m in range(TILES):
                    if first:
                        pe.wait_ge(psum_free, TILES * group + m + 1)
                    cols = slice(m * P, (m + 1) * P)
                    out = acc[:, m, 0:T]
                    for k in range(2):
                        pe.matmul(out, w_hi[:, slot, k, cols], m_hi[:, kt + k, :], start=first and k == 0, stop=False)
                        pe.matmul(out, w_hi[:, slot, k, cols], m_lo[:, kt + k, :], start=False, stop=False)
                        mm = pe.matmul(out, w_lo[:, slot, k, cols], m_hi[:, kt + k, :], start=False, stop=last and k == 1)
                    if last and m < TILES - 1:
                        mm.then_inc(tile_done, 1)
                mm.then_inc(slots_free, 1)

            def run(quad, group, n, m_hi, m_lo, s0=0, ready=None, counts=None):
                for s in range(n):
                    if ready is not None:
                        pe.wait_ge(ready, counts[s])
                    chunk(quad, s0 + s, group, s == 0, s == n - 1, m_hi, m_lo, 2 * s)

            def row_sums(norm):
                pe.wait_ge(part_ready, 4 * norm + 4)
                for q in range(4):
                    mm = pe.matmul(side[:, STATS:STATS + T], ones[:, :], part[:, q, :], start=q == 0, stop=q == 3)
                mm.then_inc(sumsq_ready, 1)

            def h_run(quad, group, s0=0, norm=0, stats=None):
                for s in range(N_MODEL):
                    pe.wait_ge(h_lo_ready, KT * norm + 2 * s + 2)
                    if stats is not None and s == 5:
                        row_sums(stats)
                    chunk(quad, s0 + s, group, s == 0, s == N_MODEL - 1, h_hi, h_lo, 2 * s)

            pe.wait_ge(ones_ready, 1)
            h_run(0, 0, stats=0)
            h_run(0, 1, s0=N_MODEL)
            h_run(0, 2, s0=2 * N_MODEL)
            with pe.Fori(1, NG) as g:
                for n in range(3):
                    h_run(6 * g, 3 * g + n, s0=n * N_MODEL)

            def turn_values(g):
                for qt in range(2):
                    bank = 2 * (g % 2) + qt
                    if g == 2:
                        pe.wait_ge(vtok_ready, qt + 1)
                    for h in range(HEADS):
                        mm = pe.transpose(side[:, 512 * bank + P * h:512 * bank + P * (h + 1)],
                                          qkv[:, 12 * g + 8 + h, P * qt:P * (qt + 1)], ident[:, :])
                    mm.then_inc(vt_done, 1)

            def scores(u):
                h, qt = u // 2, u % 2
                if u == 0:
                    pe.wait_ge(vtok_ready, 2 * NG)
                else:
                    pe.wait_ge(masked, u)
                n = P * (qt + 1)
                for g in range(NG):
                    mm = pe.matmul(side[:, SCORES + n * g:SCORES + n * (g + 1)],
                                   qkv[:, 12 * g + h, P * qt:P * (qt + 1)], qkv[:, 12 * g + 4 + h, 0:n],
                                   start=True, stop=True)
                mm.then_inc(scores_done, 1)

            def turn_probs(u):
                pe.wait_ge(prob_ready, u + 1)
                if u == 0:
                    pe.wait_ge(srow_ready, 1)
                else:
                    pe.wait_ge(att_f_ready, u)
                for b in range(NG * (u % 2 + 1)):
                    mm = pe.transpose(side[:, TURNED + P * b:TURNED + P * (b + 1)], prob[:, P * b:P * (b + 1)], ident[:, :])
                mm.then_inc(turned, 1)

            def head_out(u):
                h, kbs = u // 2, u % 2 + 1
                pe.wait_ge(prob_t_ready, u + 1)
                blocks = NG * kbs
                for b in range(blocks):
                    g, kb = b // kbs, b % kbs
                    mm = pe.matmul(side[:, HEAD_OUT:HEAD_OUT + P],
                                   vtok[:, kb, (g * HEADS + h) * HEAD_DIM:(g * HEADS + h + 1) * HEAD_DIM],
                                   prob_t[:, P * b:P * (b + 1)], start=b == 0, stop=b == blocks - 1)
                mm.then_inc(head_done, 1)

            pe.wait_ge(ident_landed, 16)
            for slot in range(6 * N_MODEL):
                if slot < NG:
                    if slot == 0:
                        pe.wait_ge(psum_free, TILES * GROUP0["ucb"] + TILES)
                    turn_values(slot)
                if slot == NG:
                    pe.wait_ge(gathered, 3)
                    pe.wait_ge(vtok_ready, 2 * (NG - 1))
                    for a in range(3):
                        mm = pe.transpose(side[0:NG * HEADS * BATCH, 1024 + HEAD_DIM * a:1024 + HEAD_DIM * (a + 1)],
                                          sgath[:, a, :], ident[:, :])
                    mm.then_inc(srow_done, 1)
                if slot == 4:
                    pe.wait_ge(roped, 2 * NG)
                for u in range(2 * HEADS):
                    if slot == 5 * u + 4:
                        scores(u)
                    if slot == 5 * u + 7:
                        turn_probs(u)
                    if slot == 5 * u + 8:
                        head_out(u)
                s = slot % N_MODEL
                chunk(QUAD0["ucb"], slot, GROUP0["ucb"] + slot // N_MODEL, s == 0, s == N_MODEL - 1, h_hi, h_lo, 2 * s)

            with pe.Fori(0, 4) as i:
                h_run(2 * i + QUAD0["gate_a"], i + GROUP0["gate_a"])
            pe.wait_ge(scored, 8)
            pe.transpose(side[0:BATCH * HEADS, 0:ROWS_A], sc_a[:, :], ident[0:ROWS_A, 0:ROWS_A]).then_inc(sturned, 1)
            pe.transpose(side[0:BATCH * HEADS, ROWS_A:SAMPLE_KEYS], sc_b[:, :], ident[0:ROWS_B, 0:ROWS_B]).then_inc(sturned, 1)
            pe.wait_ge(ab_ready, 2)
            with pe.Fori(0, 4) as i:
                run(i + QUAD0["conv_out"], i + GROUP0["conv_out"], N_CONV, ab_hi, ab_lo)
            pe.wait_ge(sprob_ready, 1)
            nbh = BATCH * HEADS
            pe.transpose(side[0:ROWS_A, 512:512 + nbh], sprob[:, 0:ROWS_A], ident[0:nbh, 0:nbh]).then_inc(spt_done, 1)
            pe.transpose(side[0:ROWS_B, 544:544 + nbh], sprob[:, ROWS_A:SAMPLE_KEYS], ident[0:nbh, 0:nbh]).then_inc(spt_done, 1)
            pe.wait_ge(v_landed, 64)
            pe.wait_ge(spt_ready, 2)
            for b in range(BATCH):
                for h in range(HEADS):
                    c, col, cols = HEADS * b + h, 1024 + BATCH * h + b, slice(h * HEAD_DIM, (h + 1) * HEAD_DIM)
                    pe.matmul(side[:, col:col + 1], v_a[:, b, cols], pt_a[:, c:c + 1], start=True, stop=False)
                    mm = pe.matmul(side[:, col:col + 1], v_b[:, b, cols], pt_b[:, c:c + 1], start=False, stop=True)
            mm.then_inc(shead_done, 1)
            with pe.Fori(0, 4) as i:
                h_run(2 * i + QUAD0["gate_b"], i + GROUP0["gate_b"])
            pe.wait_ge(att_ready, 2 * HEADS)
            pe.wait_ge(satt_ready, 1)
            with pe.Fori(0, 2) as i:
                for half in range(2):
                    run(i + QUAD0["attn_out"], 2 * i + (half + GROUP0["attn_out"]), N_ATT, att_hi, att_lo, s0=N_ATT * half)
            with pe.Fori(0, 4) as i:
                run(2 * i + QUAD0["w_out"], i + GROUP0["w_out"], N_MODEL, t_hi, t_lo,
                    ready=t_ready, counts=[s // 2 + 1 for s in range(N_MODEL)])

            def ffn_pair(half, i, stats=None):
                quad, g = 4 * i + QUAD0["ffn_" + half], 2 * i + GROUP0["ffn_" + half]
                h_run(quad, g, norm=1, stats=stats)
                h_run(quad, g + 1, s0=N_MODEL, norm=1)

            def down(half, i, n, pair0):
                quad = (2 * n // RING) * i + QUAD0["down_" + half]
                for k in range(2):
                    run(quad, 2 * i + (k + GROUP0["down_" + half]), n, f_hi, f_lo, s0=n * k,
                        ready=f_ready, counts=[pair0 + s // 2 + 1 for s in range(n)])

            ffn_pair("a", 0, stats=1)
            with pe.Fori(1, PAIRS_A) as i:
                ffn_pair("a", i)
            with pe.Fori(0, 2) as i:
                down("a", i, N_DOWN_A, 0)
            with pe.Fori(0, PAIRS_B) as i:
                ffn_pair("b", i)
            with pe.Fori(0, 2) as i:
                down("b", i, N_DOWN_B, PAIRS_A)
            row_sums(2)

        @block.gpsimd
        def _(pool):
            pool.dma_start(par[:, :], params).then_inc(par_landed, 16)
            for q in range(4):
                pool.dma_start(x_in[:, 4 * q:4 * q + 4, :], x_fm[:, 4 * q:4 * q + 4, :]).then_inc(x_landed[q], 16)
            pool.memset(ones[:, :], 1.0).then_inc(ones_ready, 1)
            pool.dma_start(rot[:, :, :], rope_tab).then_inc(rot_landed, 16)
            pool.dma_start(ident[:, :], ident_in).then_inc(ident_landed, 16)
            pool.dma_start(mask[:, :], masks).then_inc(mask_landed, 16)
            pool.dma_start(st_mix[:, :, :, :], st_mix_in).then_inc(st_landed, 16)
            pool.dma_start(st_ffn[:, :, :, :], st_ffn_in).then_inc(st_landed, 16)
            pool.memset(zb[:, :, 0:2], 0.0).then_inc(zpad_ready, 1)

            def copy_cache(b):
                for (w, _), src, dst in zip(GROUPS, caches, s_kv):
                    n = (min(w, PAST) - 1) * 2 * ATT_W
                    flat = [t.rearrange("b w n -> b (w n)") for t in (src, dst)]
                    pool.dma_start(flat[1][bass.ds(b, 1), 0:n].rearrange("b (a n) -> (b a) n", a=64),
                                   flat[0][bass.ds(b, 1), 2 * ATT_W:2 * ATT_W + n].rearrange("b (a n) -> (b a) n", a=64)
                                   ).then_inc(cache_copied, 16)

            pool.wait_ge(st_landed, 32)
            pool.wait_ge(par_landed, 16)
            for n, (state, out, tiles_n, col) in enumerate(((st_mix, base_mix, CT, PAR_CW), (st_ffn, base_ffn, FT, PAR_FW))):
                w0, w1 = (par[:, col + k * tiles_n:col + (k + 1) * tiles_n].unsqueeze(2).to_broadcast([P, tiles_n, BATCH])
                          for k in range(2))
                pool.tensor_tensor(out[:, :, :], state[:, 0], w0, ALU.mult).then_inc(base_step, 1)
                if n:
                    pool.wait_ge(base_ready, n)
                pool.tensor_tensor(tap_tmp[:, 0:tiles_n, :], state[:, 1], w1, ALU.mult).then_inc(base_step, 1)
                pool.wait_ge(base_step, 2 * n + 2)
                pool.tensor_tensor(out[:, :, :], out[:, :, :], tap_tmp[:, 0:tiles_n, :], ALU.add).then_inc(base_ready, 1)
            pool.tensor_copy(keep_mix[:, :, 2:2 + BATCH], st_mix[:, 1])
            pool.tensor_copy(keep_ffn[:, :, 2:2 + BATCH], st_ffn[:, 1])

            for b in range(2):
                pool.wait_ge(slots_free, RING + 16 + 24 * b)
                copy_cache(b)

            pool.wait_ge(psum_free, TILES * GROUP0["ucb"] + TILES)
            pool.wait_ge(roped, 2 * NG)
            for a in range(3):
                src = qkv[:, :, SEQ:T].rearrange("p (g a h) b -> p a g h b", g=NG, a=3)[:, a]
                pool.tensor_copy(sgath[:, a, :].rearrange("p (g h b) -> p g h b", g=NG, h=HEADS), src).then_inc(gathered, 1)
            for g in range(NG):
                n = min(GROUPS[g][0], SEQ)
                pool.dma_start(p_kv[g].rearrange("c d t -> d c t"), qkv[:, 12 * g + 4:12 * g + 12, SEQ - n:SEQ]).then_inc(kv_stored, 16)
            pool.wait_ge(srow_ready, 1)
            for g in range(NG):
                rows = slice(HEADS * BATCH * g, HEADS * BATCH * (g + 1))
                pool.dma_start(q_new[g].rearrange("b h d -> h b d"), srow[rows, 0, :]).then_inc(rows_sent, 16)
                for a in range(2):
                    pool.dma_start(kv_new[g, :, a].rearrange("b h d -> h b d"), srow[rows, 1 + a, :]).then_inc(rows_sent, 16)
            pool.wait_ge(rows_sent, 16 * 3 * NG)
            for g, (w, _) in enumerate(GROUPS):
                pool.dma_start(s_kv[g][:, min(w, PAST) - 1, :],
                               kv_new[g].rearrange("b a h d -> b (a h d)")).then_inc(own_out, 16)
            for j in range(2):
                wait_taken(pool, GROUP0["ucb"] + 3 * j + 1, TILES - 1)
                pool.tensor_copy(keep_mix[:, 4 * j:4 * j + 4, 0:2], zb[:, :, SEQ:SEQ + 2]).then_inc(z_kept, 1)
                pool.tensor_copy(keep_mix[:, 4 * j:4 * j + 4, 2 + BATCH:ST], zb[:, :, 2 + SEQ:2 + T]).then_inc(z_kept, 1)
            pool.wait_ge(z_kept, 4)
            pool.dma_start(conv_state_out, keep_mix[:, :, :]).then_inc(state_stored, 16)

            own = kv_new.rearrange("g b a h d -> g b a (h d)")
            cached = [c.rearrange("b w (a n) -> w b a n", a=2) for c in caches]
            q_rows = q_new.rearrange("g b h d -> g b (h d)")
            pool.wait_ge(att_ready, 2 * HEADS)
            pool.wait_ge(ab_ready, 2)
            pool.wait_ge(kv_stored, 16 * NG)
            pool.dma_start(v_a[:, :, :], cached[0][:, :, 1]).then_inc(v_landed, 16)
            pool.dma_start(v_b[0:ROW_G2], cached[1][0:PAST:GROUPS[1][1], :, 1]).then_inc(v_landed, 16)
            pool.dma_start(v_b[ROW_G2:ROW_OWN], cached[2][0:PAST:GROUPS[2][1], :, 1]).then_inc(v_landed, 16)
            pool.dma_start(v_b[ROW_OWN:ROWS_B], own[:, :, 1]).then_inc(v_landed, 16)

            def load_keys(i):
                two = bass.ds(2 * i, 2)
                pool.dma_start(k_a[:, :, :], cached[0][:, two, 0]).then_inc(kq_landed, 16)
                pool.dma_start(k_b[0:ROW_G2], cached[1][0:PAST:GROUPS[1][1], two, 0]).then_inc(kq_landed, 16)
                pool.dma_start(k_b[ROW_G2:ROW_OWN], cached[2][0:PAST:GROUPS[2][1], two, 0]).then_inc(kq_landed, 16)
                pool.dma_start(k_b[ROW_OWN:ROWS_B], own[:, two, 0]).then_inc(kq_landed, 16)
                pool.dma_start(q_a[:, :, :], q_rows[0, two].partition_broadcast(ROWS_A)).then_inc(kq_landed, 16)
                pool.dma_start(q_b[0:ROW_G2], q_rows[1, two].partition_broadcast(SAMPLE_ROWS[1])).then_inc(kq_landed, 16)
                pool.dma_start(q_b[ROW_G2:ROW_OWN], q_rows[2, two].partition_broadcast(SAMPLE_ROWS[2])).then_inc(kq_landed, 16)
                pool.dma_start(q_b[ROW_OWN:ROWS_B], q_rows[:, two]).then_inc(kq_landed, 16)

            load_keys(0)
            with pool.Fori(1, 4) as i:
                pool.wait_ge(scored, 2 * i)
                load_keys(i)

            pool.wait_ge(slots_free, RING + 4 * QUAD0["gate_b"])
            pool.dma_start(x[:, :, :], x_fm).then_inc(x_back, 16)

            def keep_ffn_state(p, group):
                wait_taken(pool, group, TILES - 1)
                pool.tensor_copy(keep_ffn[:, bass.ds(4 * p, 4), 0:2], fz[:, :, SEQ:SEQ + 2]).then_inc(fz_kept, 1)
                pool.tensor_copy(keep_ffn[:, bass.ds(4 * p, 4), 2 + BATCH:ST], fz[:, :, 2 + SEQ:2 + T]).then_inc(fz_kept, 1)

            with pool.Fori(0, PAIRS_A) as i:
                keep_ffn_state(i, 2 * i + GROUP0["ffn_a"])
                copy_cache(i + 2)
            with pool.Fori(0, PAIRS_B) as i:
                keep_ffn_state(i + PAIRS_A, 2 * i + GROUP0["ffn_b"])
            pool.wait_ge(fz_kept, 2 * (PAIRS_A + PAIRS_B))
            pool.dma_start(ffn_state_out, keep_ffn[:, :, :]).then_inc(state_stored, 16)


def rope_table():
    half = HEAD_DIM // 2
    inv = (np.float32(THETA) ** (-np.arange(half, dtype=np.float32) / half)).astype(np.float32)
    pos = np.concatenate([np.arange(SEQ), np.full(BATCH, PAST)]).astype(np.float32)
    ang = (inv[:, None] * pos[None, :]).astype(np.float64)
    cos, sin = np.cos(ang), np.sin(ang)
    return np.stack([np.concatenate([cos, cos]), np.concatenate([-sin, sin])], axis=1).astype(np.float32)


def mask_table():
    q, k = np.arange(P)[:, None], np.arange(2 * P)[None, :]
    out = []
    for qt in range(2):
        for _, d in GROUPS:
            dist = q + P * qt - k
            ok = (dist >= 0) & (dist <= SUB_WIN * d) & (dist % d == 0)
            out.append(np.where(ok, 0.0, 1e30)[:, :P * (qt + 1)])
    return np.concatenate(out, axis=1).astype(np.float32)


def kernel(**inputs):
    import concourse.bacc as _bacc
    from concourse.bass_utils import run_bass_kernel_spmd as _run

    a = {k: np.asarray(v) for k, v in inputs.items()}

    def per_feature(v):
        v = v.reshape(*v.shape[:-1], -1, P)
        return np.moveaxis(v, -1, 0)

    tokens = np.concatenate([a["x_prompt"][0], a["x_sample"][:, 0]])
    fed = {
        "x_fm": per_feature(tokens).transpose(0, 2, 1),
        "w_in": a["w_in"][0], "w_conv_out": a["w_conv_out"][0], "w_attn_out": a["w_attn_out"][0],
        "w_out": a["w_out"][0], "w_ffn_in": a["w_ffn_in"][0], "w_ffn_down": a["w_ffn_down"][0],
        "params": np.concatenate([per_feature(a[n]).reshape(P, -1) for n in (
            "norm_mix", "norm_ffn", "norm_final", "conv_mix_w", "ffn_conv_w", "ffn_conv_b")], axis=1),
        "rope_tab": rope_table(), "masks": mask_table(), "ident": np.eye(P, dtype=np.float32),
        "st_mix": per_feature(a["state_conv_mix"][0]).transpose(0, 2, 3, 1),
        "st_ffn": per_feature(a["state_conv_ffn"][0]).transpose(0, 2, 3, 1),
    }
    for g in range(NG):
        c = a[f"cache_kv_g{g + 1}"][0]
        fed[f"cache{g}"] = c.reshape(BATCH, c.shape[1], 2 * ATT_W)

    nc = _bacc.Bacc("TRN2", target_bir_lowering=False, num_devices=1)
    fed = {n: np.ascontiguousarray(v) for n, v in fed.items()}
    aps = {n: nc.dram_tensor(n, v.shape, mybir.dt.from_np(v.dtype), kind="ExternalInput").ap() for n, v in fed.items()}

    def dram(name, shape, kind="ExternalOutput"):
        return nc.dram_tensor(name, tuple(shape), F32, kind=kind).ap()

    y = dram("y_out", (P, KT, T))
    p_kv = [dram(f"p_kv{g}", (2 * HEADS, HEAD_DIM, min(w, SEQ))) for g, (w, _) in enumerate(GROUPS)]
    s_kv = [dram(f"s_kv{g}", (BATCH, min(w, PAST), 2 * ATT_W)) for g, (w, _) in enumerate(GROUPS)]
    conv_state, ffn_state = dram("conv_state", (P, CT, ST)), dram("ffn_state", (P, FT, ST))
    q_new = dram("q_new", (NG, BATCH, HEADS, HEAD_DIM), "Internal")
    kv_new = dram("kv_new", (NG, BATCH, 2, HEADS, HEAD_DIM), "Internal")
    trunk_program(nc, aps["x_fm"], aps["w_in"], aps["w_conv_out"], aps["w_attn_out"], aps["w_out"], aps["w_ffn_in"],
                  aps["w_ffn_down"], aps["params"], aps["rope_tab"], aps["masks"], aps["ident"], aps["st_mix"],
                  aps["st_ffn"], [aps[f"cache{g}"] for g in range(NG)], q_new, kv_new,
                  y, p_kv, s_kv, conv_state, ffn_state)
    got = _run(nc, [fed], core_ids=[0]).results[0]

    def token_rows(v):
        return np.asarray(v).transpose(2, 1, 0).reshape(v.shape[2], -1)

    rows = token_rows(got["y_out"])
    out = [rows[None, :SEQ], rows[SEQ:, None]]
    for g in range(NG):
        v = np.asarray(got[f"p_kv{g}"]).reshape(2, HEADS, HEAD_DIM, -1)
        out.append(v.transpose(3, 0, 1, 2)[None, None])
    states = [token_rows(got[n]) for n in ("conv_state", "ffn_state")]
    out += [s[None, None, 0:2] for s in states]
    for g in range(NG):
        v = np.asarray(got[f"s_kv{g}"])
        out.append(v.reshape(1, BATCH, v.shape[1], 2, HEADS, HEAD_DIM))
    out += [s[2:].reshape(2, BATCH, -1).transpose(1, 0, 2)[None] for s in states]
    return tuple(np.ascontiguousarray(o) for o in out)
```

```python
from contextlib import ExitStack

import numpy as np

import concourse.bass as bass
from concourse import mybir

F32 = mybir.dt.float32
F32R = mybir.dt.float32r
ALU = mybir.AluOpType
ACT = mybir.ActivationFunctionType
AX_X = mybir.AxisListType.X

P = 128
D_MODEL = 2048
D_CONV = 1024
D_FF = 5632
HEADS = 4
HEAD_DIM = 128
GROUPS = ((128, 1), (512, 4), (2048, 16))
NG = len(GROUPS)
SUB_WIN = 128
ATT_W = HEADS * HEAD_DIM
SEQ = 256
BATCH = 8
PAST = 256
T = SEQ + BATCH
EPS = 1e-6
THETA = 10000.0
SCALE = HEAD_DIM ** -0.5

KT = D_MODEL // P
CT = D_CONV // P
FT = D_FF // P
GW = 512
RING = 4
AHEAD = 3
TILES = GW // P

N_MODEL, N_CONV, N_ATT = KT // 2, CT // 2, ATT_W // P // 2
PAIRS_A, PAIRS_B = 6, 5
N_DOWN_A, N_DOWN_B = PAIRS_A * TILES // 2, PAIRS_B * TILES // 2
PHASES = (("qkv", 9, N_MODEL), ("ucb", 6, N_MODEL), ("gate_a", 4, N_MODEL), ("conv_out", 4, N_CONV),
          ("gate_b", 4, N_MODEL), ("attn_out", 4, N_ATT), ("w_out", 4, N_MODEL),
          ("ffn_a", 2 * PAIRS_A, N_MODEL), ("down_a", 4, N_DOWN_A),
          ("ffn_b", 2 * PAIRS_B, N_MODEL), ("down_b", 4, N_DOWN_B))
GROUP0, QUAD0 = {}, {}
_g = _c = 0
for _name, _n, _chunks in PHASES:
    assert _c % RING == 0
    GROUP0[_name], QUAD0[_name] = _g, _c // RING
    _g, _c = _g + _n, _c + _n * _chunks
CHUNKS = _c

SAMPLE_ROWS = tuple(min(w, PAST) // d for w, d in GROUPS)
ROWS_A = SAMPLE_ROWS[0]
ROW_G2, ROW_OWN = SAMPLE_ROWS[1], SAMPLE_ROWS[1] + SAMPLE_ROWS[2]
ROWS_B = ROW_OWN + NG
SAMPLE_KEYS = ROWS_A + ROWS_B

SCORE, EXP, NORM, TURN, OUT = 5, 6, 7, 9, 11

OUT_PIECES = ((0, 2), (2, 4), (4, 8), (8, 12), (12, 16))

STATS_CHUNK = N_MODEL + 2
WARM_UP = 12

PAR_G1, PAR_G2, PAR_GF = 0, KT, 2 * KT
PAR_CW = 3 * KT
PAR_FW = PAR_CW + 3 * CT
PAR_FB = PAR_FW + 3 * FT
PAR_N = PAR_FB + FT
MASK_N = NG * P + NG * 2 * P
ST = 2 + 2 * BATCH


def trunk_program(nc, x_fm, w_in, w_conv_out, w_attn_out, w_out, w_ffn_in, w_ffn_down, params, rope_tab,
                  masks, own_heads_in, ident_in, st_mix_in, st_ffn_in, caches, q_new, kv_new,
                  y_out, p_kv, s_kv, conv_state_out, ffn_state_out):
    with ExitStack() as ctx:
        def sem(name):
            return ctx.enter_context(nc.semaphore(name))

        base = -(-nc.sbuf_base // 64) * 64
        size = {F32: 4, F32R: 4}
        cursor = [base]

        def place(name, shape, dt=F32, at=None):
            off = cursor[0] if at is None else at
            n = size[dt] * int(np.prod(shape[1:]))
            t = nc.alloc_sbuf_tensor_at(name, list(shape), dt, offset=off)
            if at is None:
                cursor[0] = off + -(-n // 32) * 32
            return t

        raw = place("raw", [P, RING, 2, GW])
        w_hi = place("w_hi", [P, RING, 2, GW], F32R)
        w_lo = place("w_lo", [P, RING, 2, GW], F32R)
        h_at = cursor[0]
        h_hi = place("h_hi", [P, KT, T], F32R)
        h_lo = place("h_lo", [P, KT, T], F32R)
        rot_at = cursor[0]
        rot = place("rot", [P, 2, T])
        rot_r = place("rot_r", [P, 2, T])
        r = place("r", [P, T])
        r2 = place("r2", [P, T])
        part = place("part", [P, 2, T])
        par = place("par", [P, PAR_N])
        ident = place("ident", [P, P])
        ones = place("ones", [P, P])
        st_at = cursor[0]
        st_mix = place("st_mix", [P, 2, CT, BATCH])
        st_ffn = place("st_ffn", [P, 2, FT, BATCH])
        base_mix = place("base_mix", [P, CT, BATCH])
        base_ffn = place("base_ffn", [P, FT, BATCH])
        tap_tmp = place("tap_tmp", [P, FT, BATCH])
        keep_mix = place("keep_mix", [P, CT, ST])
        keep_ffn = place("keep_ffn", [P, FT, ST])
        sc_a = place("sc_a", [ROWS_A, BATCH * HEADS])
        sc_b = place("sc_b", [ROWS_B, BATCH * HEADS])
        own_heads = place("own_heads", [BATCH * HEADS, HEADS])
        small = place("small", [P, 4, 2 * HEADS])
        ssmall = place("ssmall", [BATCH * HEADS, 4])
        att_tmp = place("att_tmp", [P, HEADS * BATCH])
        sprob = place("sprob", [BATCH * HEADS, SAMPLE_KEYS])
        ab_at = cursor[0]
        ab_hi = place("ab_hi", [P, CT, T], F32R)
        ab_lo = place("ab_lo", [P, CT, T], F32R)
        x_in = place("x_in", [P, KT, T], at=ab_at)
        x = place("x", [P, KT, T], at=ab_at)
        att_hi = place("att_hi", [P, HEADS, T], F32R)
        att_lo = place("att_lo", [P, HEADS, T], F32R)
        zone = cursor[0]
        qkv = place("qkv", [P, 3 * NG * HEADS, T])
        sq0 = place("sq0", [P, KT, T], at=zone + 4 * 12 * T)
        vtok = place("vtok", [P, 2, NG * HEADS * HEAD_DIM])
        mask = place("mask", [P, MASK_N])
        tmp_at = cursor[0]
        qraw = place("qraw", [P, HEADS, T])
        qswap = place("qswap", [P, HEADS, T])
        prob = place("prob", [P, NG * 2 * P], at=tmp_at)
        prob_t = place("prob_t", [P, NG * 2 * P], at=tmp_at + 4 * NG * 2 * P)
        ub = place("ub", [P, TILES, T])
        zb = place("zb", [P, TILES, T + 2])
        yb = place("yb", [P, TILES, T])
        att_f = place("att_f", [P, P])
        sgath = place("sgath", [P, 3, NG * HEADS * BATCH])
        srow = place("srow", [NG * HEADS * BATCH, 3, HEAD_DIM])
        end_b = cursor[0]
        cursor[0] = zone
        gate_a = place("gate_a", [P, KT, T])
        gate_b = place("gate_b", [P, KT, T])
        mix_at = cursor[0]
        v_a = place("v_a", [ROWS_A, BATCH, ATT_W])
        v_b = place("v_b", [ROWS_B, BATCH, ATT_W])
        k_a = place("k_a", [ROWS_A, 2, ATT_W], at=mix_at - 4 * KT * T)
        k_b = place("k_b", [ROWS_B, 2, ATT_W], at=mix_at - 4 * KT * T + 8 * ATT_W)
        q_a = place("q_a", [ROWS_A, 2, ATT_W], at=mix_at - 4 * KT * T + 16 * ATT_W)
        pt_a = place("pt_a", [ROWS_A, BATCH * (HEADS * BATCH + HEADS)])
        pt_b = place("pt_b", [ROWS_B, BATCH * (HEADS * BATCH + HEADS)])
        sall = place("sall", [BATCH * HEADS, HEADS, HEAD_DIM], at=st_at)
        srows = place("srows", [BATCH * HEADS, HEAD_DIM], at=st_at + 4 * ATT_W)
        q_b = place("q_b", [ROWS_B, 2, ATT_W], at=rot_at)
        end_c = cursor[0]
        cursor[0] = mix_at
        t_hi = place("t_hi", [P, KT, T], F32R)
        t_lo = place("t_lo", [P, KT, T], F32R)
        tf = place("tf", [P, 2, TILES, T])
        sq = place("sq", [P, TILES, T])
        end_d = cursor[0]
        cursor[0] = zone
        f_hi = place("f_hi", [P, TILES * PAIRS_A, T], F32R)
        f_lo = place("f_lo", [P, TILES * PAIRS_A, T], F32R)
        fz = place("fz", [P, TILES, T + 2])
        fy = place("fy", [P, TILES, T])
        ff = place("ff", [P, TILES, T])
        fsq = place("fsq", [P, TILES, T])
        yg = place("yg", [P, KT, T], at=h_at)
        end_e = cursor[0]
        assert max(end_b, end_c, end_d, end_e) <= nc.sbuf_usable_end, (end_b, end_c, end_d, end_e, nc.sbuf_usable_end)

        acc = ctx.enter_context(nc.psum_tensor("acc", [P, TILES, 512], F32))
        side = ctx.enter_context(nc.psum_tensor("side", [P, 4 * 512], F32))
        SCORES, TURNED, HEAD_OUT = 0, 2 * 512, 3 * 512 + 256
        STATS = 3 * 512

        holds = sem("holds")
        raw_landed = [sem(f"raw_landed{i}") for i in range(RING)]
        hi_ready, lo_ready = sem("hi_ready"), sem("lo_ready")
        half_landed, half_hi, half_lo = sem("half_landed"), sem("half_hi"), sem("half_lo")
        slots_free = sem("slots_free")
        tile_done = sem("tile_done")
        psum_free = sem("psum_free")
        x_landed = [sem(f"x_landed{i}") for i in range(KT // 2)]
        par_landed, rot_landed, mask_landed, ident_landed, st_landed = (
            sem("par_landed"), sem("rot_landed"), sem("mask_landed"), sem("ident_landed"), sem("st_landed"))
        last_squared = sem("last_squared")
        h_hi_ready, h_lo_ready, squared, part_ready = sem("h_hi_ready"), sem("h_lo_ready"), sem("squared"), sem("part_ready")
        four_summed, part_cleared = sem("four_summed"), sem("part_cleared")
        sumsq_ready, ms_ready, r2_ready, r_ready = sem("sumsq_ready"), sem("ms_ready"), sem("r2_ready"), sem("r_ready")
        ones_ready, zpad_ready = sem("ones_ready"), sem("zpad_ready")
        rot_r_ready, swapped, rope_parts, roped = sem("rot_r_ready"), sem("swapped"), sem("rope_parts"), sem("roped")
        vt_done, vtok_ready = sem("vt_done"), sem("vtok_ready")
        scores_done, masked, negmax_ready, exp_ready, rsum_ready, prob_ready = (
            sem("scores_done"), sem("masked"), sem("negmax_ready"), sem("exp_ready"), sem("rsum_ready"), sem("prob_ready"))
        turned, prob_t_ready, head_done, att_f_ready, att_hi_ready, att_ready = (
            sem("turned"), sem("prob_t_ready"), sem("head_done"), sem("att_f_ready"), sem("att_hi_ready"), sem("att_ready"))
        tap2, tap1, conv_y, conv_yr, ab_hi_ready, ab_ready, z_kept = (
            sem("tap2"), sem("tap1"), sem("conv_y"), sem("conv_yr"), sem("ab_hi_ready"), sem("ab_ready"), sem("z_kept"))
        base_step, base_ready = sem("base_step"), sem("base_ready")
        gathered, srow_done, srow_ready, rows_sent, own_out = (
            sem("gathered"), sem("srow_done"), sem("srow_ready"), sem("rows_sent"), sem("own_out"))
        v_landed, kq_landed, prod_ready, scored = sem("v_landed"), sem("kq_landed"), sem("prod_ready"), sem("scored")
        sturned, snegated, smax_ready, sexp_ready, srsum_ready, sprob_ready, spt_done, spt_ready, shead_done = (
            sem("sturned"), sem("snegated"), sem("smax_ready"), sem("sexp_ready"), sem("srsum_ready"),
            sem("sprob_ready"), sem("spt_done"), sem("spt_ready"), sem("shead_done"))
        own_heads_landed, pt_zeroed, picked, srows_ready, sturned_back = (
            sem("own_heads_landed"), sem("pt_zeroed"), sem("picked"), sem("srows_ready"), sem("sturned_back"))
        satt_f, satt_hi, satt_ready = sem("satt_f"), sem("satt_hi"), sem("satt_ready")
        gate_a_ready, gate_b_ready = sem("gate_a_ready"), sem("gate_b_ready")
        mixed, t_hi_ready, t_ready, x_back = sem("mixed"), sem("t_hi_ready"), sem("t_ready"), sem("x_back")
        fz_kept, ftap2, ftap1, fconv, fsilu, fscaled, f_hi_ready, f_ready = (
            sem("fz_kept"), sem("ftap2"), sem("ftap1"), sem("fconv"), sem("fsilu"), sem("fscaled"),
            sem("f_hi_ready"), sem("f_ready"))
        yg_ready, y_ready = sem("yg_ready"), sem("y_ready")
        kv_stored, cache_copied, state_stored, y_stored = sem("kv_stored"), sem("cache_copied"), sem("state_stored"), sem("y_stored")

        def wait_tile(eng, group, quad, n, m):
            if m < TILES - 1:
                eng.wait_ge(tile_done, (TILES - 1) * group + m + 1)
            else:
                eng.wait_ge(slots_free, 4 * quad + RING + n)

        def wait_taken(eng, group, m):
            eng.wait_ge(psum_free, TILES * group + TILES + m + 1)

        def held(eng):
            eng.sem_inc(holds, 1)

        def tiles(t, first, n=1):
            return t[:, bass.ds(first, n), :]

        def over_tiles(row, n=TILES):
            return row.unsqueeze(1).to_broadcast([P, n, T])

        def par_col(col):
            return par[:, bass.ds(col, 1)]

        def fetched_loop(engine, start, end):
            return nc.Fori(start, end, engines=(engine,), hint_back_edge=True)

        block = ctx.enter_context(nc.Block())

        @block.sync
        def _(sp):
            sp.dma_start(par[:, :], params).then_inc(par_landed, 16)

            def load(weights, k0, col, quad, s, wait=True):
                if wait:
                    sp.wait_ge(lo_ready, 4 * quad + s - RING + 1)
                    held(sp)
                src = weights[k0 * P:(k0 + 2) * P, bass.ds(col, GW)].rearrange("(k p) n -> p k n", p=P)
                sp.dma_start(raw[:, s % RING], src).then_inc(raw_landed[s % RING], 16)

            def group(weights, n, col, quad, s0=0, k0=0):
                for s in range(n):
                    load(weights, k0 + 2 * s, col, quad, s0 + s)

            qkv_col = 3 * D_CONV
            for q in range(KT // 2):
                sp.dma_start(x_in[:, 2 * q:2 * q + 2, :], x_fm[:, 2 * q:2 * q + 2, :]).then_inc(x_landed[q], 16)
                if q == 0:
                    for k, landed in enumerate((half_landed, raw_landed[0])):
                        sp.dma_start(raw[:, 0, k], w_in[k * P:(k + 1) * P, qkv_col:qkv_col + GW]).then_inc(landed, 16)
                elif q < RING:
                    load(w_in, 2 * q, qkv_col, 0, q, wait=False)
            for s in range(RING, N_MODEL):
                load(w_in, 2 * s, qkv_col, 0, s)
            with sp.Fori(1, 9) as i:
                group(w_in, N_MODEL, GW * i + qkv_col, 2 * i)
            for i in range(6):
                col = (0, 2 * D_CONV, D_CONV)[i % 3] + GW * (i // 3)
                group(w_in, N_MODEL, col, QUAD0["ucb"] + 2 * i)
            gate_col = 3 * D_CONV + 9 * ATT_W
            with sp.Fori(0, 4) as i:
                group(w_in, N_MODEL, GW * i + gate_col, 2 * i + QUAD0["gate_a"])
            with sp.Fori(0, 4) as i:
                group(w_conv_out, N_CONV, GW * i, i + QUAD0["conv_out"])
            with sp.Fori(0, 4) as i:
                group(w_in, N_MODEL, GW * i + (gate_col + D_MODEL), 2 * i + QUAD0["gate_b"])
            with sp.Fori(0, 2) as i:
                group(w_attn_out, N_ATT, 2 * GW * i, i + QUAD0["attn_out"])
                group(w_attn_out, N_ATT, 2 * GW * i + GW, i + QUAD0["attn_out"], s0=N_ATT)
            with sp.Fori(0, 4) as i:
                group(w_out, N_MODEL, GW * i, 2 * i + QUAD0["w_out"])
            for half, pairs, n, first in (("a", PAIRS_A, N_DOWN_A, 0), ("b", PAIRS_B, N_DOWN_B, PAIRS_A)):
                with sp.Fori(0, pairs) as i:
                    group(w_ffn_in, N_MODEL, GW * i + (D_FF + GW * first), 4 * i + QUAD0["ffn_" + half])
                    group(w_ffn_in, N_MODEL, GW * i + GW * first, 4 * i + QUAD0["ffn_" + half], s0=N_MODEL)
                with sp.Fori(0, 2) as i:
                    quad = (2 * n // RING) * i + QUAD0["down_" + half]
                    group(w_ffn_down, n, 2 * GW * i, quad, k0=TILES * first)
                    group(w_ffn_down, n, 2 * GW * i + GW, quad, s0=n, k0=TILES * first)
            for n, (q0, q1) in enumerate(OUT_PIECES):
                sp.wait_ge(y_ready, n + 1)
                sp.dma_start(y_out[:, q0:q1, :], yg[:, q0:q1, :]).then_inc(y_stored, 16)
            sp.wait_ge(y_stored, 16 * len(OUT_PIECES))
            sp.wait_ge(kv_stored, 16 * NG)
            sp.wait_ge(own_out, 16 * NG)
            sp.wait_ge(cache_copied, 16 * NG * BATCH)
            sp.wait_ge(state_stored, 32)

        @block.scalar
        def _(act):
            def hi(quad, s):
                act.wait_ge(raw_landed[s % RING], 16 * quad + 16 * (s // RING + 1))
                act.wait_ge(slots_free, 4 * quad + s + 1)
                act.activation(w_hi[:, s % RING], raw[:, s % RING], ACT.Copy).then_inc(hi_ready, 1)

            def his(quad, s0, s1):
                for s in range(s0 + AHEAD, s1 + AHEAD):
                    hi(quad, s)

            def split_rows(norm, src, first, par0, n=TILES):
                for m in range(n):
                    if norm:
                        wait_taken(act, first["group"], m)
                        held(act)
                    act.activation(tiles(h_hi, first["tile"] + m), tiles(src, first["tile"] + m), ACT.Copy,
                                   scale=par_col(first["tile"] + (par0 + m))).then_inc(h_hi_ready, 1)

            def inverse_root(norm):
                act.wait_ge(r2_ready, norm + 1)
                act.activation(r[:, :], r2[:, :], ACT.Sqrt).then_inc(r_ready, 1)

            act.wait_ge(ones_ready, 1)
            act.activation(small[:, 3, 0:1], ones[:, 0:1], ACT.Copy)
            act.wait_ge(par_landed, 16)
            for q in range(KT // 2):
                act.wait_ge(x_landed[q], 16)
                split_rows(0, x_in, {"tile": 2 * q}, PAR_G1, 2)
                if q == 0:
                    for k, landed, ready in ((0, half_landed, half_hi), (1, raw_landed[0], hi_ready)):
                        act.wait_ge(landed, 16)
                        act.activation(w_hi[:, 0, k], raw[:, 0, k], ACT.Copy).then_inc(ready, 1)
                elif q < RING:
                    hi(0, q)
            hi(0, RING)
            for q in range(4):
                hi(0, RING + 1 + q)
                act.activation(sq0[:, 4 * q:4 * q + 4, :], x_in[:, 4 * q:4 * q + 4, :], ACT.Square).then_inc(squared, 1)

            def rope_inputs(group, unit, wait):
                for m in range(TILES):
                    wait_tile(act, group, 2 * group, N_MODEL, m)
                    if m == 0 and wait:
                        act.wait_ge(roped, unit)
                    act.activation(qraw[:, m, :], acc[:, m, 0:T], ACT.Copy).then_inc(psum_free, 1)
                wait_taken(act, group, TILES - 1)
                for dst, src in ((0, 64), (64, 0)):
                    act.activation(qswap[dst:dst + 64, :, :], qraw[src:src + 64, :, :], ACT.Copy).then_inc(swapped, 1)

            def qkv_body(g, peeled):
                his(6 * g, RING + 5 - AHEAD if peeled else 0, N_MODEL)
                rope_inputs(3 * g, 2 * g, not peeled)
                if peeled:
                    his(6 * g, N_MODEL, STATS_CHUNK + 1)
                    inverse_root(0)
                    his(6 * g, STATS_CHUNK + 1, 2 * N_MODEL)
                else:
                    his(6 * g, N_MODEL, 2 * N_MODEL)
                rope_inputs(3 * g + 1, 2 * g + 1, True)
                his(6 * g, 2 * N_MODEL, 3 * N_MODEL)

            qkv_body(0, True)
            with fetched_loop(mybir.EngineType.Activation, 1, NG) as g:
                qkv_body(g, False)

            def exp_unit(u):
                h, qt = u // 2, u % 2
                n = NG * P * (qt + 1)
                act.wait_ge(negmax_ready, u + 1)
                act.activation(prob[:, 0:n], prob[:, 0:n], ACT.Exp, bias=small[:, 0, u:u + 1], scale=-1.0,
                               accum_out=small[:, 1, u:u + 1]).then_inc(exp_ready, 1)

            def probs_out(u):
                n = NG * P * (u % 2 + 1)
                act.wait_ge(turned, u + 1)
                act.activation(prob_t[:, 0:n], side[:, TURNED:TURNED + n], ACT.Copy).then_inc(prob_t_ready, 1)

            for slot in range(6 * N_MODEL):
                hi(QUAD0["ucb"], slot + AHEAD)
                if 2 <= slot <= NG + 1:
                    g = slot - 2
                    for qt in range(2):
                        act.wait_ge(vt_done, 2 * g + qt + 1)
                        bank = 2 * (g % 2) + qt
                        act.activation(vtok[:, qt, g * ATT_W:(g + 1) * ATT_W],
                                       side[:, 512 * bank:512 * (bank + 1)], ACT.Copy).then_inc(vtok_ready, 1)
                if slot == NG + 1:
                    act.wait_ge(srow_done, 1)
                    act.activation(srow[:, :, :].rearrange("p a d -> p (a d)"),
                                   side[0:NG * HEADS * BATCH, 1024:1024 + 3 * HEAD_DIM], ACT.Copy).then_inc(srow_ready, 1)
                for j in range(2):
                    if slot == 24 * j + 17:
                        for m in range(TILES):
                            wait_taken(act, GROUP0["ucb"] + 3 * j + 1, m)
                            act.activation(yb[:, m, :], zb[:, m, 2:2 + T], ACT.Copy,
                                           scale=par_col(PAR_CW + 2 * CT + 4 * j + m)).then_inc(tap2, 1)
                    if slot == 24 * j + 23:
                        wait_taken(act, GROUP0["ucb"] + 3 * j + 2, TILES - 1)
                        act.activation(ab_hi[:, 4 * j:4 * j + 4, :], ub[:, :, :], ACT.Copy).then_inc(ab_hi_ready, 1)
                for u in range(2 * HEADS):
                    if slot == 5 * u + EXP:
                        exp_unit(u)
                    if slot == 5 * u + TURN:
                        probs_out(u)

            def gate(name, i, out, ready, early=0):
                his(2 * i + QUAD0[name], 0, N_MODEL + early)
                wait_taken(act, i + GROUP0[name], TILES - 1)
                held(act)
                act.activation(tiles(out, 4 * i, 4), tiles(out, 4 * i, 4), ACT.Sigmoid).then_inc(ready, 1)

            with fetched_loop(mybir.EngineType.Activation, 0, 4) as i:
                gate("gate_a", i, gate_a, gate_a_ready)
            act.wait_ge(smax_ready, 1)
            act.activation(sprob[:, :], sprob[:, :], ACT.Exp, bias=ssmall[:, 0:1], scale=-1.0,
                           accum_out=ssmall[:, 1:2]).then_inc(sexp_ready, 1)
            with fetched_loop(mybir.EngineType.Activation, 0, 3) as i:
                his(i + QUAD0["conv_out"], 0, N_CONV)
            act.wait_ge(pt_zeroed, 2)
            act.wait_ge(spt_done, 2)
            for out, rows, col in ((pt_a, ROWS_A, 512), (pt_b, ROWS_B, 544)):
                act.activation(out[:, :].rearrange("p (b c) -> p b c", b=BATCH)[:, :, 0:HEADS],
                               side[0:rows, col:col + BATCH * HEADS].rearrange("p (b h) -> p b h", b=BATCH),
                               ACT.Copy).then_inc(spt_ready, 1)
            his(3 + QUAD0["conv_out"], 0, N_CONV)
            with fetched_loop(mybir.EngineType.Activation, 0, 3) as i:
                gate("gate_b", i, gate_b, gate_b_ready)
            gate("gate_b", 3, gate_b, gate_b_ready, early=1)

            def mix_hi(j):
                act.wait_ge(mixed, j + 1)
                act.activation(t_hi[:, 4 * j:4 * j + 4, :], tf[:, j % 2], ACT.Copy).then_inc(t_hi_ready, 1)

            for j in range(4):
                if j:
                    his(QUAD0["attn_out"], N_ATT * j, N_ATT * j + 1)
                    mix_hi(j - 1)
                his(QUAD0["attn_out"], N_ATT * j + 1, N_ATT * (j + 1))
            mix_hi(3)
            with fetched_loop(mybir.EngineType.Activation, 0, 4) as i:
                his(2 * i + QUAD0["w_out"], 0, N_MODEL)
                split_rows(1, x, {"tile": 4 * i, "group": i + GROUP0["w_out"]}, PAR_G2)
                act.wait_ge(part_ready, i + 4)
                held(act)
                act.activation(sq[:, :, :], tiles(x, 4 * i, 4), ACT.Square).then_inc(squared, 1)

            def ffn_pair(half, pair0, i, peeled):
                quad, g = 4 * i + QUAD0["ffn_" + half], 2 * i + GROUP0["ffn_" + half]
                p = i + pair0
                his(quad, 0, 7)
                if peeled:
                    inverse_root(1)
                his(quad, 7, N_MODEL)
                for m in range(TILES):
                    wait_taken(act, g, m)
                    held(act)
                    act.activation(fy[:, m, :], fz[:, m, 2:2 + T], ACT.Identity, bias=par_col(4 * p + (PAR_FB + m)),
                                   scale=par_col(4 * p + (PAR_FW + 2 * FT + m))).then_inc(ftap2, 1)
                his(quad, N_MODEL, N_MODEL + 4)
                act.wait_ge(fconv, 5 * p + 5)
                act.activation(fy[:, :, :], fy[:, :, :], ACT.Silu).then_inc(fsilu, 1)
                his(quad, N_MODEL + 4, 2 * N_MODEL)
                wait_taken(act, g + 1, TILES - 1)
                held(act)
                act.activation(tiles(f_hi, 4 * i, 4), ff[:, :, :], ACT.Copy).then_inc(f_hi_ready, 1)

            ffn_pair("a", 0, 0, True)
            with fetched_loop(mybir.EngineType.Activation, 1, PAIRS_A) as i:
                ffn_pair("a", 0, i, False)
            with fetched_loop(mybir.EngineType.Activation, 0, 2) as i:
                his((2 * N_DOWN_A // RING) * i + QUAD0["down_a"], 0, 2 * N_DOWN_A)
            with fetched_loop(mybir.EngineType.Activation, 0, PAIRS_B) as i:
                ffn_pair("b", PAIRS_A, i, False)
            for j in range(4):
                quad = QUAD0["down_b"] + (2 * N_DOWN_B // RING) * (j // 2)
                s0 = N_DOWN_B * (j % 2)
                his(quad, s0, s0 + N_DOWN_B - (AHEAD if j == 3 else 0))
                act.wait_ge(part_ready, 8 + j)
                for m in range(TILES):
                    wait_taken(act, GROUP0["down_b"] + j, m)
                    sq_m = act.activation(fsq[:, m, :], x[:, 4 * j + m, :], ACT.Square)
                    if j == 3:
                        sq_m.then_inc(last_squared, 1)
                    elif m == TILES - 1:
                        sq_m.then_inc(squared, 1)
                for m in range(TILES):
                    act.activation(yg[:, 4 * j + m, :], x[:, 4 * j + m, :], ACT.Copy,
                                   scale=par_col(PAR_GF + 4 * j + m)).then_inc(yg_ready, 1)
            inverse_root(2)

        @block.vector
        def _(dve):
            def lo(quad, s):
                dve.wait_ge(hi_ready, 4 * quad + s + 1)
                dve.tensor_tensor(w_lo[:, s % RING], raw[:, s % RING], w_hi[:, s % RING].bitcast(F32),
                                  ALU.subtract).then_inc(lo_ready, 1)

            def los(quad, s0, s1):
                for s in range(s0 + AHEAD, s1 + AHEAD):
                    lo(quad, s)

            def take_tiles(take, quad=None, s=None):
                for m in range(TILES):
                    if m == 1 and s is not None:
                        los(quad, s, s + 1)
                    take(m)

            def split_rows(src, tile, ready0, par0, n=TILES):
                for m in range(n):
                    dve.wait_ge(h_hi_ready, tile + (ready0 + m + 1))
                    dve.scalar_tensor_tensor(tiles(h_lo, tile + m), tiles(src, tile + m), par_col(tile + (par0 + m)),
                                             tiles(h_hi, tile + m).bitcast(F32), ALU.mult,
                                             ALU.subtract).then_inc(h_lo_ready, 1)

            def sum_squares(squares, norm, q):
                dve.wait_ge(squared, q + (4 * norm + 1))
                if norm or q:
                    dve.wait_ge(part_ready, q + 4 * norm)
                dve.tensor_reduce(part[:, 1, :], squares.rearrange("p m t -> p t m"), AX_X, ALU.add).then_inc(four_summed, 1)
                dve.wait_ge(four_summed, q + (4 * norm + 1))
                dve.tensor_tensor(part[:, 0, :], part[:, 0, :], part[:, 1, :], ALU.add).then_inc(part_ready, 1)

            def clear_sum(norm):
                dve.memset(part[:, 0, :], 0.0).then_inc(part_cleared, 1)
                dve.wait_ge(part_cleared, norm + 1)

            def row_factor(norm):
                dve.wait_ge(sumsq_ready, norm + 1)
                dve.tensor_scalar(r2[:, :], side[:, STATS:STATS + T], 1.0 / D_MODEL, EPS, ALU.mult,
                                  ALU.add).then_inc(ms_ready, 1)
                dve.wait_ge(ms_ready, norm + 1)
                dve.reciprocal(r2[:, :], r2[:, :]).then_inc(r2_ready, 1)

            clear_sum(0)
            dve.wait_ge(par_landed, 16)
            for q in range(KT // 2):
                split_rows(x_in, 2 * q, 0, PAR_G1, 2)
                if q == 0:
                    for k, ready, done in ((0, half_hi, half_lo), (1, hi_ready, lo_ready)):
                        dve.wait_ge(ready, 1)
                        dve.tensor_tensor(w_lo[:, 0, k], raw[:, 0, k], w_hi[:, 0, k].bitcast(F32), ALU.subtract).then_inc(done, 1)
                elif q < RING:
                    lo(0, q)

            def rope(unit, first):
                out = tiles(qkv, first, 4)
                dve.wait_ge(swapped, 2 * unit + 2)
                dve.tensor_tensor(out, qraw[:, :, :], over_tiles(rot_r[:, 0, :]), ALU.mult).then_inc(rope_parts, 1)
                dve.tensor_tensor(qswap[:, :, :], qswap[:, :, :], over_tiles(rot_r[:, 1, :]), ALU.mult).then_inc(rope_parts, 1)
                dve.wait_ge(rope_parts, 2 * unit + 2)
                dve.tensor_tensor(out, out, qswap[:, :, :], ALU.add).then_inc(roped, 1)

            def qkv_body(g, peeled):
                quad = 6 * g
                if peeled:
                    lo(quad, RING)
                    for q in range(4):
                        lo(quad, RING + 1 + q)
                        sum_squares(sq0[:, 4 * q:4 * q + 4, :], 0, q)
                    los(quad, RING + 5 - AHEAD, STATS_CHUNK)
                    row_factor(0)
                    los(quad, STATS_CHUNK, STATS_CHUNK + 1)
                    dve.wait_ge(r_ready, 1)
                    dve.wait_ge(rot_landed, 16)
                    dve.tensor_tensor(rot_r[:, :, :], rot[:, :, :], over_tiles(r[:, :], 2), ALU.mult).then_inc(rot_r_ready, 1)
                    los(quad, STATS_CHUNK + 1, N_MODEL + 4)
                    dve.wait_ge(rot_r_ready, 1)
                else:
                    los(quad, 0, N_MODEL + 4)
                rope(2 * g, 12 * g)
                los(quad, N_MODEL + 4, 2 * N_MODEL + 4)
                rope(2 * g + 1, 12 * g + 4)
                los(quad, 2 * N_MODEL + 4, 3 * N_MODEL - 1)

                def take_v(m):
                    wait_tile(dve, 3 * g + 2, quad, 3 * N_MODEL, m)
                    dve.tensor_tensor(tiles(qkv, 12 * g + 8 + m), acc[:, m:m + 1, 0:T], over_tiles(r[:, :], 1),
                                      ALU.mult).then_inc(psum_free, 1)

                take_tiles(take_v, quad, 3 * N_MODEL - 1)

            qkv_body(0, True)
            with fetched_loop(mybir.EngineType.DVE, 1, NG) as g:
                qkv_body(g, False)

            dve.wait_ge(mask_landed, 16)
            for slot in range(6 * N_MODEL):
                if slot % N_MODEL < N_MODEL - 1:
                    los(QUAD0["ucb"], slot, slot + 1)
                group, j = GROUP0["ucb"] + slot // N_MODEL, slot // 24
                if slot == 24 * j + 7:
                    def take_u(m):
                        wait_tile(dve, group, 2 * group, N_MODEL, m)
                        dve.tensor_tensor(ub[:, m, :], acc[:, m, 0:T], r2[:, :], ALU.mult).then_inc(psum_free, 1)

                    take_tiles(take_u, QUAD0["ucb"], slot)
                if slot == 24 * j + 15:
                    dve.wait_ge(zpad_ready, 1)
                    if j:
                        dve.wait_ge(z_kept, 2)
                    wait_taken(dve, group - 1, TILES - 1)

                    def take_c(m):
                        wait_tile(dve, group, 2 * group, N_MODEL, m)
                        dve.tensor_tensor(zb[:, m, 2:2 + T], acc[:, m, 0:T], ub[:, m, :], ALU.mult).then_inc(psum_free, 1)

                    take_tiles(take_c, QUAD0["ucb"], slot)
                for u in range(2 * HEADS):
                    h, qt = u // 2, u % 2
                    n = NG * P * (qt + 1)
                    if slot == 5 * u + SCORE:
                        dve.wait_ge(scores_done, u + 1)
                        m0 = NG * P * qt
                        if u >= 1:
                            dve.wait_ge(turned, u)
                        dve.scalar_tensor_tensor(prob[:, 0:n], side[:, SCORES:SCORES + n], -SCALE, mask[:, m0:m0 + n],
                                                 ALU.mult, ALU.add).then_inc(masked, 1)
                        dve.wait_ge(masked, u + 1)
                        dve.tensor_reduce(small[:, 0, u:u + 1], prob[:, 0:n], AX_X, ALU.min).then_inc(negmax_ready, 1)
                    if slot == 5 * u + NORM:
                        dve.wait_ge(exp_ready, u + 1)
                        dve.reciprocal(small[:, 2, u:u + 1], small[:, 1, u:u + 1]).then_inc(rsum_ready, 1)
                        dve.wait_ge(rsum_ready, u + 1)
                        dve.tensor_scalar(prob[:, 0:n], prob[:, 0:n], small[:, 2, u:u + 1], None,
                                          ALU.mult).then_inc(prob_ready, 1)
                    if slot == 5 * u + OUT:
                        cols = slice(qt * P, (qt + 1) * P)
                        dve.wait_ge(head_done, u + 1)
                        dve.tensor_copy(att_f[:, :], side[:, HEAD_OUT:HEAD_OUT + P]).then_inc(att_f_ready, 1)
                        dve.wait_ge(att_f_ready, u + 1)
                        dve.tensor_copy(att_hi[:, h, cols], att_f[:, :]).then_inc(att_hi_ready, 1)
                        dve.wait_ge(att_hi_ready, u + 1)
                        dve.tensor_tensor(att_lo[:, h, cols], att_f[:, :], att_hi[:, h, cols].bitcast(F32),
                                          ALU.subtract).then_inc(att_ready, 1)
                if slot == 24 * j + 18:
                    for m in range(TILES):
                        dve.wait_ge(tap2, 4 * j + m + 1)
                        dve.scalar_tensor_tensor(yb[:, m, 0:SEQ], zb[:, m, 1:1 + SEQ], par_col(PAR_CW + CT + 4 * j + m),
                                                 yb[:, m, 0:SEQ], ALU.mult, ALU.add).then_inc(tap1, 1)
                if slot == 24 * j + 19:
                    for m in range(TILES):
                        dve.wait_ge(tap1, 4 * j + m + 1)
                        dve.scalar_tensor_tensor(yb[:, m, 0:SEQ], zb[:, m, 0:SEQ], par_col(PAR_CW + 4 * j + m),
                                                 yb[:, m, 0:SEQ], ALU.mult, ALU.add).then_inc(conv_y, 1)
                    dve.wait_ge(base_ready, 1)
                    dve.tensor_tensor(yb[:, :, SEQ:T], yb[:, :, SEQ:T], base_mix[:, 4 * j:4 * j + 4, :],
                                      ALU.add).then_inc(conv_y, 1)
                if slot == 24 * j + 20:
                    dve.wait_ge(conv_y, 5 * j + 5)
                    dve.tensor_tensor(yb[:, :, :], yb[:, :, :], over_tiles(r[:, :]), ALU.mult).then_inc(conv_yr, 1)
                if slot == 24 * j + 23:
                    dve.wait_ge(conv_yr, j + 1)

                    def take_b(m):
                        wait_tile(dve, group, 2 * group, N_MODEL, m)
                        dve.tensor_tensor(ub[:, m, :], acc[:, m, 0:T], yb[:, m, :], ALU.mult).then_inc(psum_free, 1)

                    take_tiles(take_b, QUAD0["ucb"], slot)
                    dve.wait_ge(ab_hi_ready, j + 1)
                    dve.tensor_tensor(ab_lo[:, 4 * j:4 * j + 4, :], ub[:, :, :], ab_hi[:, 4 * j:4 * j + 4, :].bitcast(F32),
                                      ALU.subtract).then_inc(ab_ready, 1)

            def take_gate(name, i, out):
                def take(m):
                    wait_tile(dve, i + GROUP0[name], 2 * i + QUAD0[name], N_MODEL, m)
                    dve.tensor_tensor(tiles(out, 4 * i + m), acc[:, m:m + 1, 0:T], over_tiles(r[:, :], 1),
                                      ALU.mult).then_inc(psum_free, 1)

                take_tiles(take, 2 * i + QUAD0[name], N_MODEL - 1)

            dve.wait_ge(kv_stored, 16 * NG)
            dve.wait_ge(rows_sent, 16 * 3 * NG)
            with fetched_loop(mybir.EngineType.DVE, 0, 4) as i:
                quad = 2 * i + QUAD0["gate_a"]
                los(quad, 0, 4)
                dve.wait_ge(kq_landed, 128 * i + 128)
                dve.tensor_tensor(k_a[:, :, :], k_a[:, :, :], q_a[:, :, :], ALU.mult).then_inc(prod_ready, 1)
                los(quad, 4, 5)
                dve.tensor_tensor(k_b[:, :, :], k_b[:, :, :], q_b[:, :, :], ALU.mult).then_inc(prod_ready, 1)
                for n, (out, prod) in enumerate(((sc_a, k_a), (sc_b, k_b))):
                    los(quad, 5 + n, 6 + n)
                    dve.wait_ge(prod_ready, 2 * i + 1 + n)
                    dve.tensor_reduce(out[:, bass.ds(2 * HEADS * i, 2 * HEADS)],
                                      prod[:, :, :].rearrange("p b (h d) -> p (b h) d", h=HEADS),
                                      AX_X, ALU.add).then_inc(scored, 1)
                take_gate("gate_a", i, gate_a)
            dve.wait_ge(sturned, 2)
            dve.tensor_scalar(sprob[:, :], side[0:BATCH * HEADS, 0:SAMPLE_KEYS], -SCALE, None, ALU.mult).then_inc(snegated, 1)
            dve.wait_ge(snegated, 1)
            dve.tensor_reduce(ssmall[:, 0:1], sprob[:, :], AX_X, ALU.min).then_inc(smax_ready, 1)
            dve.wait_ge(sexp_ready, 1)
            dve.reciprocal(ssmall[:, 2:3], ssmall[:, 1:2]).then_inc(srsum_ready, 1)
            dve.wait_ge(srsum_ready, 1)
            dve.tensor_scalar(sprob[:, :], sprob[:, :], ssmall[:, 2:3], None, ALU.mult).then_inc(sprob_ready, 1)
            with fetched_loop(mybir.EngineType.DVE, 0, 4) as i:
                los(i + QUAD0["conv_out"], 0, N_CONV - 1)
                dve.wait_ge(gate_a_ready, 4)

                def take_a(m):
                    wait_tile(dve, i + GROUP0["conv_out"], i + QUAD0["conv_out"], N_CONV, m)
                    dve.tensor_tensor(tiles(gate_a, 4 * i + m), acc[:, m:m + 1, 0:T], tiles(gate_a, 4 * i + m),
                                      ALU.mult).then_inc(psum_free, 1)

                take_tiles(take_a, i + QUAD0["conv_out"], N_CONV - 1)
            los(QUAD0["gate_b"], 0, 7)
            dve.wait_ge(own_heads_landed, 16)
            dve.wait_ge(base_ready, 2)
            dve.wait_ge(shead_done, 1)
            dve.tensor_tensor(sall[:, :, :], side[0:BATCH * HEADS, 1024:1024 + ATT_W].rearrange("p (h d) -> p h d", h=HEADS),
                              own_heads[:, :].unsqueeze(2).to_broadcast([BATCH * HEADS, HEADS, HEAD_DIM]),
                              ALU.mult).then_inc(picked, 1)
            dve.wait_ge(picked, 1)
            dve.tensor_reduce(srows[:, :], sall[:, :, :].rearrange("p h d -> p d h"), AX_X, ALU.add).then_inc(srows_ready, 1)
            take_gate("gate_b", 0, gate_b)
            with fetched_loop(mybir.EngineType.DVE, 1, 3) as i:
                los(2 * i + QUAD0["gate_b"], 0, N_MODEL - 1)
                take_gate("gate_b", i, gate_b)
            los(2 * 3 + QUAD0["gate_b"], 0, 4)
            dve.wait_ge(sturned_back, 1)
            sout = side[:, 0:HEADS * BATCH].rearrange("p (b h) -> p h b", h=HEADS)
            satt = att_tmp[:, :].rearrange("p (h b) -> p h b", h=HEADS)
            dve.tensor_copy(satt, sout).then_inc(satt_f, 1)
            dve.wait_ge(satt_f, 1)
            dve.tensor_copy(att_hi[:, :, SEQ:T], satt).then_inc(satt_hi, 1)
            dve.wait_ge(satt_hi, 1)
            dve.tensor_tensor(att_lo[:, :, SEQ:T], satt, att_hi[:, :, SEQ:T].bitcast(F32), ALU.subtract).then_inc(satt_ready, 1)
            los(2 * 3 + QUAD0["gate_b"], 4, N_MODEL - 1)
            take_gate("gate_b", 3, gate_b)
            for j in range(4):
                los(QUAD0["attn_out"], N_ATT * j, N_ATT * (j + 1) - 1)
                g = GROUP0["attn_out"] + j
                if j == 0:
                    dve.wait_ge(gate_b_ready, 4)
                if j >= 2:
                    dve.wait_ge(t_ready, j - 1)

                def take_mixed(m):
                    wait_tile(dve, g, QUAD0["attn_out"], N_ATT * (j + 1), m)
                    dve.tensor_tensor(tf[:, j % 2, m, :], acc[:, m, 0:T], gate_b[:, 4 * j + m, :], ALU.mult).then_inc(psum_free, 1)

                take_tiles(take_mixed, QUAD0["attn_out"], N_ATT * (j + 1) - 1)
                wait_taken(dve, g, TILES - 1)
                dve.tensor_tensor(tf[:, j % 2], tf[:, j % 2], gate_a[:, 4 * j:4 * j + 4, :], ALU.add).then_inc(mixed, 1)

            def add_to_x(tile, group, quad, n, last=False):
                def take(m):
                    wait_tile(dve, group, quad, n, m)
                    dve.tensor_tensor(tiles(x, tile + m), acc[:, m:m + 1, 0:T], tiles(x, tile + m),
                                      ALU.add).then_inc(psum_free, 1)

                take_tiles(take, quad, None if last else n - 1)

            dve.wait_ge(x_back, 16)
            clear_sum(1)
            with fetched_loop(mybir.EngineType.DVE, 0, 4) as i:
                los(2 * i + QUAD0["w_out"], 0, N_MODEL - 1)
                add_to_x(4 * i, i + GROUP0["w_out"], 2 * i + QUAD0["w_out"], N_MODEL)
                split_rows(x, 4 * i, KT, PAR_G2)
                sum_squares(sq[:, :, :], 1, i)

            def ffn_pair(half, pair0, i, peeled):
                quad, g = 4 * i + QUAD0["ffn_" + half], 2 * i + GROUP0["ffn_" + half]
                p = i + pair0
                los(quad, 0, 6)
                if peeled:
                    row_factor(1)
                los(quad, 6, N_MODEL - 1)
                if peeled:
                    dve.wait_ge(r_ready, 2)
                else:
                    dve.wait_ge(fz_kept, 2 * p)

                def take_gate_group(m):
                    wait_tile(dve, g, quad, N_MODEL, m)
                    dve.tensor_tensor(fz[:, m, 2:2 + T], acc[:, m, 0:T], r[:, :], ALU.mult).then_inc(psum_free, 1)

                take_tiles(take_gate_group, quad, N_MODEL - 1)
                los(quad, N_MODEL, N_MODEL + 2)
                for m in range(TILES):
                    dve.wait_ge(ftap2, 4 * p + m + 1)
                    dve.scalar_tensor_tensor(fy[:, m, 0:SEQ], fz[:, m, 1:1 + SEQ], par_col(4 * p + (PAR_FW + FT + m)),
                                             fy[:, m, 0:SEQ], ALU.mult, ALU.add).then_inc(ftap1, 1)
                los(quad, N_MODEL + 2, N_MODEL + 3)
                for m in range(TILES):
                    dve.wait_ge(ftap1, 4 * p + m + 1)
                    dve.scalar_tensor_tensor(fy[:, m, 0:SEQ], fz[:, m, 0:SEQ], par_col(4 * p + (PAR_FW + m)),
                                             fy[:, m, 0:SEQ], ALU.mult, ALU.add).then_inc(fconv, 1)
                dve.tensor_tensor(fy[:, :, SEQ:T], fy[:, :, SEQ:T], tiles(base_ffn, 4 * p, 4), ALU.add).then_inc(fconv, 1)
                los(quad, N_MODEL + 3, N_MODEL + 5)
                dve.wait_ge(fsilu, p + 1)
                dve.tensor_tensor(fy[:, :, :], fy[:, :, :], over_tiles(r[:, :]), ALU.mult).then_inc(fscaled, 1)
                los(quad, N_MODEL + 5, 2 * N_MODEL - 1)
                dve.wait_ge(fscaled, p + 1)

                def take_up_group(m):
                    wait_tile(dve, g + 1, quad, 2 * N_MODEL, m)
                    dve.tensor_tensor(ff[:, m, :], acc[:, m, 0:T], fy[:, m, :], ALU.mult).then_inc(psum_free, 1)

                take_tiles(take_up_group, quad, 2 * N_MODEL - 1)
                dve.wait_ge(f_hi_ready, p + 1)
                dve.tensor_tensor(tiles(f_lo, 4 * i, 4), ff[:, :, :], tiles(f_hi, 4 * i, 4).bitcast(F32),
                                  ALU.subtract).then_inc(f_ready, 1)

            dve.memset(fz[:, :, 0:2], 0.0).then_inc(zpad_ready, 1)
            dve.wait_ge(base_ready, 2)
            dve.wait_ge(zpad_ready, 2)
            ffn_pair("a", 0, 0, True)
            with fetched_loop(mybir.EngineType.DVE, 1, PAIRS_A) as i:
                ffn_pair("a", 0, i, False)
            with fetched_loop(mybir.EngineType.DVE, 0, 2) as i:
                quad = (2 * N_DOWN_A // RING) * i + QUAD0["down_a"]
                for half in range(2):
                    los(quad, N_DOWN_A * half, N_DOWN_A * (half + 1) - 1)
                    add_to_x(8 * i + 4 * half, 2 * i + (half + GROUP0["down_a"]), quad, N_DOWN_A * (half + 1))
            with fetched_loop(mybir.EngineType.DVE, 0, PAIRS_B) as i:
                ffn_pair("b", PAIRS_A, i, False)
            clear_sum(2)
            for j in range(4):
                quad = QUAD0["down_b"] + (2 * N_DOWN_B // RING) * (j // 2)
                s0 = N_DOWN_B * (j % 2)
                los(quad, s0, s0 + N_DOWN_B - (AHEAD if j == 3 else 1))
                add_to_x(4 * j, GROUP0["down_b"] + j, quad, s0 + N_DOWN_B, last=j == 3)
                if j < 3:
                    sum_squares(fsq[:, :, :], 2, j)
            row_factor(2)
            dve.wait_ge(r_ready, 3)
            for q0, q1 in OUT_PIECES:
                dve.wait_ge(yg_ready, q1)
                dve.tensor_tensor(yg[:, q0:q1, :], yg[:, q0:q1, :], over_tiles(r[:, :], q1 - q0),
                                  ALU.mult).then_inc(y_ready, 1)

        @block.tensor
        def _(pe):
            pe.sem_inc(slots_free, RING)
            pe.sem_inc(psum_free, TILES)

            def chunk(quad, s, group, first, last, m_hi, m_lo, kt):
                pe.wait_ge(lo_ready, 4 * quad + s + 1)
                slot = s % RING
                for m in range(TILES):
                    if first:
                        pe.wait_ge(psum_free, TILES * group + m + 1)
                    cols = slice(m * P, (m + 1) * P)
                    out = acc[:, m, 0:T]
                    for k in range(2):
                        pe.matmul(out, w_hi[:, slot, k, cols], m_hi[:, kt + k, :], start=first and k == 0, stop=False)
                        pe.matmul(out, w_hi[:, slot, k, cols], m_lo[:, kt + k, :], start=False, stop=False)
                        mm = pe.matmul(out, w_lo[:, slot, k, cols], m_hi[:, kt + k, :], start=False, stop=last and k == 1)
                    if last and m < TILES - 1:
                        mm.then_inc(tile_done, 1)
                mm.then_inc(slots_free, 1)

            def first_chunk():
                for k, done in enumerate((half_lo, lo_ready)):
                    pe.wait_ge(done, 1)
                    pe.wait_ge(h_lo_ready, k + 1)
                    for m in range(TILES):
                        cols = slice(m * P, (m + 1) * P)
                        if k == 0:
                            pe.wait_ge(psum_free, m + 1)
                        pe.matmul(acc[:, m, 0:T], w_hi[:, 0, k, cols], h_hi[:, k, :], start=k == 0, stop=False)
                        pe.matmul(acc[:, m, 0:T], w_hi[:, 0, k, cols], h_lo[:, k, :], start=False, stop=False)
                        mm = pe.matmul(acc[:, m, 0:T], w_lo[:, 0, k, cols], h_hi[:, k, :], start=False, stop=False)
                mm.then_inc(slots_free, 1)

            def run(quad, group, n, m_hi, m_lo, s0=0, ready=None, counts=None):
                for s in range(n):
                    if ready is not None:
                        pe.wait_ge(ready, counts[s])
                    chunk(quad, s0 + s, group, s == 0, s == n - 1, m_hi, m_lo, 2 * s)

            def row_sums(norm):
                pe.wait_ge(part_ready, 4 * norm + 4)
                pe.matmul(side[:, STATS:STATS + T], ones[:, :], part[:, 0, :], start=True, stop=True).then_inc(sumsq_ready, 1)

            def h_run(quad, group, s0=0, norm=0, stats=None, stats_at=6, start=0):
                for s in range(start, N_MODEL):
                    pe.wait_ge(h_lo_ready, KT * norm + 2 * s + 2)
                    if stats is not None and s == stats_at:
                        row_sums(stats)
                    chunk(quad, s0 + s, group, s == 0, s == N_MODEL - 1, h_hi, h_lo, 2 * s)

            pe.wait_ge(ones_ready, 1)
            for _ in range(WARM_UP):
                pe.matmul(side[:, 0:P], ones[:, :], ones[:, :], start=True, stop=True)
            first_chunk()
            h_run(0, 0, start=1)
            h_run(0, 1, s0=N_MODEL, stats=0, stats_at=STATS_CHUNK - 1 - N_MODEL)
            h_run(0, 2, s0=2 * N_MODEL)
            with fetched_loop(mybir.EngineType.PE, 1, NG) as g:
                for n in range(3):
                    h_run(6 * g, 3 * g + n, s0=n * N_MODEL)

            def turn_values(g):
                for qt in range(2):
                    bank = 2 * (g % 2) + qt
                    if g == 2:
                        pe.wait_ge(vtok_ready, qt + 1)
                    for h in range(HEADS):
                        mm = pe.transpose(side[:, 512 * bank + P * h:512 * bank + P * (h + 1)],
                                          qkv[:, 12 * g + 8 + h, P * qt:P * (qt + 1)], ident[:, :])
                    mm.then_inc(vt_done, 1)

            def scores(u):
                h, qt = u // 2, u % 2
                if u == 0:
                    pe.wait_ge(vtok_ready, 2 * NG)
                    pe.wait_ge(roped, 2 * NG)
                else:
                    pe.wait_ge(masked, u)
                n = P * (qt + 1)
                for g in range(NG):
                    mm = pe.matmul(side[:, SCORES + n * g:SCORES + n * (g + 1)],
                                   qkv[:, 12 * g + h, P * qt:P * (qt + 1)], qkv[:, 12 * g + 4 + h, 0:n],
                                   start=True, stop=True)
                mm.then_inc(scores_done, 1)

            def turn_probs(u):
                pe.wait_ge(prob_ready, u + 1)
                if u == 0:
                    pe.wait_ge(srow_ready, 1)
                else:
                    pe.wait_ge(att_f_ready, u)
                for b in range(NG * (u % 2 + 1)):
                    mm = pe.transpose(side[:, TURNED + P * b:TURNED + P * (b + 1)], prob[:, P * b:P * (b + 1)], ident[:, :])
                mm.then_inc(turned, 1)

            def head_out(u):
                h, kbs = u // 2, u % 2 + 1
                pe.wait_ge(prob_t_ready, u + 1)
                blocks = NG * kbs
                for b in range(blocks):
                    g, kb = b // kbs, b % kbs
                    mm = pe.matmul(side[:, HEAD_OUT:HEAD_OUT + P],
                                   vtok[:, kb, (g * HEADS + h) * HEAD_DIM:(g * HEADS + h + 1) * HEAD_DIM],
                                   prob_t[:, P * b:P * (b + 1)], start=b == 0, stop=b == blocks - 1)
                mm.then_inc(head_done, 1)

            pe.wait_ge(ident_landed, 16)
            for slot in range(6 * N_MODEL):
                if 2 <= slot <= NG + 1:
                    if slot == 2:
                        pe.wait_ge(psum_free, TILES * GROUP0["ucb"] + TILES)
                    turn_values(slot - 2)
                if slot == NG + 1:
                    pe.wait_ge(gathered, 3)
                    pe.wait_ge(vtok_ready, 2 * (NG - 1))
                    for a in range(3):
                        mm = pe.transpose(side[0:NG * HEADS * BATCH, 1024 + HEAD_DIM * a:1024 + HEAD_DIM * (a + 1)],
                                          sgath[:, a, :], ident[:, :])
                    mm.then_inc(srow_done, 1)
                for u in range(2 * HEADS):
                    if slot == 5 * u + SCORE:
                        scores(u)
                    if slot == 5 * u + TURN:
                        turn_probs(u)
                    if slot == 5 * u + OUT:
                        head_out(u)
                s = slot % N_MODEL
                chunk(QUAD0["ucb"], slot, GROUP0["ucb"] + slot // N_MODEL, s == 0, s == N_MODEL - 1, h_hi, h_lo, 2 * s)

            with fetched_loop(mybir.EngineType.PE, 0, 4) as i:
                h_run(2 * i + QUAD0["gate_a"], i + GROUP0["gate_a"])
            pe.wait_ge(scored, 8)
            pe.transpose(side[0:BATCH * HEADS, 0:ROWS_A], sc_a[:, :], ident[0:ROWS_A, 0:ROWS_A]).then_inc(sturned, 1)
            pe.transpose(side[0:BATCH * HEADS, ROWS_A:SAMPLE_KEYS], sc_b[:, :], ident[0:ROWS_B, 0:ROWS_B]).then_inc(sturned, 1)
            pe.wait_ge(ab_ready, 2)
            with fetched_loop(mybir.EngineType.PE, 0, 3) as i:
                run(i + QUAD0["conv_out"], i + GROUP0["conv_out"], N_CONV, ab_hi, ab_lo)
            pe.wait_ge(sprob_ready, 1)
            nbh = BATCH * HEADS
            pe.transpose(side[0:ROWS_A, 512:512 + nbh], sprob[:, 0:ROWS_A], ident[0:nbh, 0:nbh]).then_inc(spt_done, 1)
            pe.transpose(side[0:ROWS_B, 544:544 + nbh], sprob[:, ROWS_A:SAMPLE_KEYS], ident[0:nbh, 0:nbh]).then_inc(spt_done, 1)
            run(3 + QUAD0["conv_out"], 3 + GROUP0["conv_out"], N_CONV, ab_hi, ab_lo)
            pe.wait_ge(v_landed, 16 * 4 * BATCH // 2)
            pe.wait_ge(spt_ready, 2)
            for b in range(BATCH):
                for n, (pt, v) in enumerate(((pt_a, v_a), (pt_b, v_b))):
                    mm = pe.matmul(side[0:nbh, 1024:1024 + ATT_W], pt[:, nbh * b:nbh * (b + 1)], v[:, b, :],
                                   start=b + n == 0, stop=b + n == BATCH)
            mm.then_inc(shead_done, 1)
            with fetched_loop(mybir.EngineType.PE, 0, 3) as i:
                h_run(2 * i + QUAD0["gate_b"], i + GROUP0["gate_b"])
            pe.wait_ge(srows_ready, 1)
            pe.transpose(side[:, 0:nbh], srows[:, :], ident[0:nbh, 0:nbh]).then_inc(sturned_back, 1)
            h_run(2 * 3 + QUAD0["gate_b"], 3 + GROUP0["gate_b"])
            pe.wait_ge(att_ready, 2 * HEADS)
            pe.wait_ge(satt_ready, 1)
            for j in range(4):
                run(QUAD0["attn_out"], GROUP0["attn_out"] + j, N_ATT, att_hi, att_lo, s0=N_ATT * j)
            with fetched_loop(mybir.EngineType.PE, 0, 4) as i:
                run(2 * i + QUAD0["w_out"], i + GROUP0["w_out"], N_MODEL, t_hi, t_lo,
                    ready=t_ready, counts=[s // 2 + 1 for s in range(N_MODEL)])

            def ffn_pair(half, i, stats=None):
                quad, g = 4 * i + QUAD0["ffn_" + half], 2 * i + GROUP0["ffn_" + half]
                h_run(quad, g, norm=1, stats=stats)
                h_run(quad, g + 1, s0=N_MODEL, norm=1)

            def down(half, i, n, pair0):
                quad = (2 * n // RING) * i + QUAD0["down_" + half]
                for k in range(2):
                    run(quad, 2 * i + (k + GROUP0["down_" + half]), n, f_hi, f_lo, s0=n * k,
                        ready=f_ready, counts=[pair0 + s // 2 + 1 for s in range(n)])

            ffn_pair("a", 0, stats=1)
            with fetched_loop(mybir.EngineType.PE, 1, PAIRS_A) as i:
                ffn_pair("a", i)
            with fetched_loop(mybir.EngineType.PE, 0, 2) as i:
                down("a", i, N_DOWN_A, 0)
            with fetched_loop(mybir.EngineType.PE, 0, PAIRS_B) as i:
                ffn_pair("b", i)
            with fetched_loop(mybir.EngineType.PE, 0, 2) as i:
                down("b", i, N_DOWN_B, PAIRS_A)
            pe.wait_ge(part_ready, 11)
            pe.matmul(side[:, STATS:STATS + T], ones[:, :], part[:, 0, :], start=True, stop=False)
            for m in range(TILES):
                pe.wait_ge(last_squared, m + 1)
                mm = pe.matmul(side[:, STATS:STATS + T], ones[:, :], fsq[:, m, :], start=False, stop=m == TILES - 1)
            mm.then_inc(sumsq_ready, 1)

        @block.gpsimd
        def _(pool):
            pool.memset(ones[:, :], 1.0).then_inc(ones_ready, 1)
            pool.memset(zb[:, :, 0:2], 0.0).then_inc(zpad_ready, 1)
            pool.wait_ge(x_landed[-1], 16)
            pool.dma_start(rot[:, :, :], rope_tab).then_inc(rot_landed, 16)
            pool.dma_start(ident[:, :], ident_in).then_inc(ident_landed, 16)
            pool.dma_start(own_heads[:, :], own_heads_in).then_inc(own_heads_landed, 16)
            pool.dma_start(mask[:, :], masks).then_inc(mask_landed, 16)
            pool.dma_start(st_mix[:, :, :, :], st_mix_in).then_inc(st_landed, 16)
            pool.dma_start(st_ffn[:, :, :, :], st_ffn_in).then_inc(st_landed, 16)

            def copy_cache(b):
                for (w, _), src, dst in zip(GROUPS, caches, s_kv):
                    n = (min(w, PAST) - 1) * 2 * ATT_W
                    flat = [t.rearrange("b w n -> b (w n)") for t in (src, dst)]
                    pool.dma_start(flat[1][bass.ds(b, 1), 0:n].rearrange("b (a n) -> (b a) n", a=64),
                                   flat[0][bass.ds(b, 1), 2 * ATT_W:2 * ATT_W + n].rearrange("b (a n) -> (b a) n", a=64)
                                   ).then_inc(cache_copied, 16)

            pool.wait_ge(st_landed, 32)
            pool.wait_ge(par_landed, 16)
            for n, (state, out, tiles_n, col) in enumerate(((st_mix, base_mix, CT, PAR_CW), (st_ffn, base_ffn, FT, PAR_FW))):
                w0, w1 = (par[:, col + k * tiles_n:col + (k + 1) * tiles_n].unsqueeze(2).to_broadcast([P, tiles_n, BATCH])
                          for k in range(2))
                pool.tensor_tensor(out[:, :, :], state[:, 0], w0, ALU.mult).then_inc(base_step, 1)
                if n:
                    pool.wait_ge(base_ready, n)
                pool.tensor_tensor(tap_tmp[:, 0:tiles_n, :], state[:, 1], w1, ALU.mult).then_inc(base_step, 1)
                pool.wait_ge(base_step, 2 * n + 2)
                pool.tensor_tensor(out[:, :, :], out[:, :, :], tap_tmp[:, 0:tiles_n, :], ALU.add).then_inc(base_ready, 1)
            pool.tensor_copy(keep_mix[:, :, 2:2 + BATCH], st_mix[:, 1])
            pool.tensor_copy(keep_ffn[:, :, 2:2 + BATCH], st_ffn[:, 1])

            for b in range(2):
                pool.wait_ge(slots_free, RING + 16 + 24 * b)
                copy_cache(b)

            pool.wait_ge(psum_free, TILES * GROUP0["ucb"] + TILES)
            pool.wait_ge(roped, 2 * NG)
            for a in range(3):
                src = qkv[:, :, SEQ:T].rearrange("p (g a h) b -> p a g h b", g=NG, a=3)[:, a]
                pool.tensor_copy(sgath[:, a, :].rearrange("p (g h b) -> p g h b", g=NG, h=HEADS), src).then_inc(gathered, 1)
            for g in range(NG):
                n = min(GROUPS[g][0], SEQ)
                pool.dma_start(p_kv[g].rearrange("c d t -> d c t"), qkv[:, 12 * g + 4:12 * g + 12, SEQ - n:SEQ]).then_inc(kv_stored, 16)
            pool.wait_ge(srow_ready, 1)
            for g in range(NG):
                rows = slice(HEADS * BATCH * g, HEADS * BATCH * (g + 1))
                pool.dma_start(q_new[g].rearrange("b h d -> h b d"), srow[rows, 0, :]).then_inc(rows_sent, 16)
                for a in range(2):
                    pool.dma_start(kv_new[g, :, a].rearrange("b h d -> h b d"), srow[rows, 1 + a, :]).then_inc(rows_sent, 16)
            pool.wait_ge(rows_sent, 16 * 3 * NG)
            for g, (w, _) in enumerate(GROUPS):
                pool.dma_start(s_kv[g][:, min(w, PAST) - 1, :],
                               kv_new[g].rearrange("b a h d -> b (a h d)")).then_inc(own_out, 16)
            for j in range(2):
                wait_taken(pool, GROUP0["ucb"] + 3 * j + 1, TILES - 1)
                pool.tensor_copy(keep_mix[:, 4 * j:4 * j + 4, 0:2], zb[:, :, SEQ:SEQ + 2]).then_inc(z_kept, 1)
                pool.tensor_copy(keep_mix[:, 4 * j:4 * j + 4, 2 + BATCH:ST], zb[:, :, 2 + SEQ:2 + T]).then_inc(z_kept, 1)
            pool.wait_ge(z_kept, 4)
            pool.dma_start(conv_state_out, keep_mix[:, :, :]).then_inc(state_stored, 16)

            own = kv_new.rearrange("g b a h d -> g b a (h d)")
            cached = [c.rearrange("b w (a n) -> w b a n", a=2) for c in caches]
            q_rows = q_new.rearrange("g b h d -> g b (h d)")

            def load_keys(i):
                two = bass.ds(2 * i, 2)
                pool.dma_start(k_a[:, :, :], cached[0][:, two, 0]).then_inc(kq_landed, 16)
                pool.dma_start(k_b[0:ROW_G2], cached[1][0:PAST:GROUPS[1][1], two, 0]).then_inc(kq_landed, 16)
                pool.dma_start(k_b[ROW_G2:ROW_OWN], cached[2][0:PAST:GROUPS[2][1], two, 0]).then_inc(kq_landed, 16)
                pool.dma_start(k_b[ROW_OWN:ROWS_B], own[:, two, 0]).then_inc(kq_landed, 16)
                pool.dma_start(q_a[:, :, :], q_rows[0, two].partition_broadcast(ROWS_A)).then_inc(kq_landed, 16)
                pool.dma_start(q_b[0:ROW_G2], q_rows[1, two].partition_broadcast(SAMPLE_ROWS[1])).then_inc(kq_landed, 16)
                pool.dma_start(q_b[ROW_G2:ROW_OWN], q_rows[2, two].partition_broadcast(SAMPLE_ROWS[2])).then_inc(kq_landed, 16)
                pool.dma_start(q_b[ROW_OWN:ROWS_B], q_rows[:, two]).then_inc(kq_landed, 16)

            def load_values(i):
                two = bass.ds(2 * i, 2)
                pool.dma_start(v_a[:, two], cached[0][:, two, 1]).then_inc(v_landed, 16)
                pool.dma_start(v_b[0:ROW_G2, two], cached[1][0:PAST:GROUPS[1][1], two, 1]).then_inc(v_landed, 16)
                pool.dma_start(v_b[ROW_G2:ROW_OWN, two], cached[2][0:PAST:GROUPS[2][1], two, 1]).then_inc(v_landed, 16)
                pool.dma_start(v_b[ROW_OWN:ROWS_B, two], own[:, two, 1]).then_inc(v_landed, 16)

            pool.wait_ge(scores_done, 2 * HEADS)
            pool.wait_ge(kv_stored, 16 * NG)
            load_keys(0)
            pool.wait_ge(att_ready, 2 * HEADS)
            pool.wait_ge(ab_ready, 2)
            pool.memset(pt_a[:, :], 0.0).then_inc(pt_zeroed, 1)
            pool.memset(pt_b[:, :], 0.0).then_inc(pt_zeroed, 1)
            load_values(0)
            with pool.Fori(1, 4) as i:
                pool.wait_ge(scored, 2 * i)
                load_keys(i)
                load_values(i)

            pool.wait_ge(slots_free, RING + 4 * QUAD0["gate_b"])
            pool.dma_start(x[:, :, :], x_fm).then_inc(x_back, 16)

            for j in range(4):
                pool.wait_ge(t_hi_ready, j + 1)
                pool.tensor_tensor(t_lo[:, 4 * j:4 * j + 4, :], tf[:, j % 2], t_hi[:, 4 * j:4 * j + 4, :].bitcast(F32),
                                   ALU.subtract).then_inc(t_ready, 1)

            def keep_ffn_state(p, group):
                wait_taken(pool, group, TILES - 1)
                pool.tensor_copy(keep_ffn[:, bass.ds(4 * p, 4), 0:2], fz[:, :, SEQ:SEQ + 2]).then_inc(fz_kept, 1)
                pool.tensor_copy(keep_ffn[:, bass.ds(4 * p, 4), 2 + BATCH:ST], fz[:, :, 2 + SEQ:2 + T]).then_inc(fz_kept, 1)

            with pool.Fori(0, PAIRS_A) as i:
                keep_ffn_state(i, 2 * i + GROUP0["ffn_a"])
                copy_cache(i + 2)
            with pool.Fori(0, PAIRS_B) as i:
                keep_ffn_state(i + PAIRS_A, 2 * i + GROUP0["ffn_b"])
            pool.wait_ge(fz_kept, 2 * (PAIRS_A + PAIRS_B))
            pool.dma_start(ffn_state_out, keep_ffn[:, :, :]).then_inc(state_stored, 16)


def rope_table():
    half = HEAD_DIM // 2
    inv = (np.float32(THETA) ** (-np.arange(half, dtype=np.float32) / half)).astype(np.float32)
    pos = np.concatenate([np.arange(SEQ), np.full(BATCH, PAST)]).astype(np.float32)
    ang = (inv[:, None] * pos[None, :]).astype(np.float64)
    cos, sin = np.cos(ang), np.sin(ang)
    return np.stack([np.concatenate([cos, cos]), np.concatenate([-sin, sin])], axis=1).astype(np.float32)


def mask_table():
    q, k = np.arange(P)[:, None], np.arange(2 * P)[None, :]
    out = []
    for qt in range(2):
        for _, d in GROUPS:
            dist = q + P * qt - k
            ok = (dist >= 0) & (dist <= SUB_WIN * d) & (dist % d == 0)
            out.append(np.where(ok, 0.0, 1e30)[:, :P * (qt + 1)])
    return np.concatenate(out, axis=1).astype(np.float32)


def kernel(**inputs):
    import concourse.bacc as _bacc
    from concourse.bass_utils import run_bass_kernel_spmd as _run

    a = {k: np.asarray(v) for k, v in inputs.items()}

    def per_feature(v):
        v = v.reshape(*v.shape[:-1], -1, P)
        return np.moveaxis(v, -1, 0)

    tokens = np.concatenate([a["x_prompt"][0], a["x_sample"][:, 0]])
    fed = {
        "x_fm": per_feature(tokens).transpose(0, 2, 1),
        "w_in": a["w_in"][0], "w_conv_out": a["w_conv_out"][0], "w_attn_out": a["w_attn_out"][0],
        "w_out": a["w_out"][0], "w_ffn_in": a["w_ffn_in"][0], "w_ffn_down": a["w_ffn_down"][0],
        "params": np.concatenate([per_feature(a[n]).reshape(P, -1) for n in (
            "norm_mix", "norm_ffn", "norm_final", "conv_mix_w", "ffn_conv_w", "ffn_conv_b")], axis=1),
        "rope_tab": rope_table(), "masks": mask_table(), "ident": np.eye(P, dtype=np.float32),
        "own_heads": np.tile(np.eye(HEADS, dtype=np.float32), (BATCH, 1)),
        "st_mix": per_feature(a["state_conv_mix"][0]).transpose(0, 2, 3, 1),
        "st_ffn": per_feature(a["state_conv_ffn"][0]).transpose(0, 2, 3, 1),
    }
    for g in range(NG):
        c = a[f"cache_kv_g{g + 1}"][0]
        fed[f"cache{g}"] = c.reshape(BATCH, c.shape[1], 2 * ATT_W)

    nc = _bacc.Bacc("TRN2", target_bir_lowering=False, num_devices=1)
    fed = {n: np.ascontiguousarray(v) for n, v in fed.items()}
    aps = {n: nc.dram_tensor(n, v.shape, mybir.dt.from_np(v.dtype), kind="ExternalInput").ap() for n, v in fed.items()}

    def dram(name, shape, kind="ExternalOutput"):
        return nc.dram_tensor(name, tuple(shape), F32, kind=kind).ap()

    y = dram("y_out", (P, KT, T))
    p_kv = [dram(f"p_kv{g}", (2 * HEADS, HEAD_DIM, min(w, SEQ))) for g, (w, _) in enumerate(GROUPS)]
    s_kv = [dram(f"s_kv{g}", (BATCH, min(w, PAST), 2 * ATT_W)) for g, (w, _) in enumerate(GROUPS)]
    conv_state, ffn_state = dram("conv_state", (P, CT, ST)), dram("ffn_state", (P, FT, ST))
    q_new = dram("q_new", (NG, BATCH, HEADS, HEAD_DIM), "Internal")
    kv_new = dram("kv_new", (NG, BATCH, 2, HEADS, HEAD_DIM), "Internal")
    trunk_program(nc, aps["x_fm"], aps["w_in"], aps["w_conv_out"], aps["w_attn_out"], aps["w_out"], aps["w_ffn_in"],
                  aps["w_ffn_down"], aps["params"], aps["rope_tab"], aps["masks"], aps["own_heads"], aps["ident"], aps["st_mix"],
                  aps["st_ffn"], [aps[f"cache{g}"] for g in range(NG)], q_new, kv_new,
                  y, p_kv, s_kv, conv_state, ffn_state)
    got = _run(nc, [fed], core_ids=[0]).results[0]

    def token_rows(v):
        return np.asarray(v).transpose(2, 1, 0).reshape(v.shape[2], -1)

    rows = token_rows(got["y_out"])
    out = [rows[None, :SEQ], rows[SEQ:, None]]
    for g in range(NG):
        v = np.asarray(got[f"p_kv{g}"]).reshape(2, HEADS, HEAD_DIM, -1)
        out.append(v.transpose(3, 0, 1, 2)[None, None])
    states = [token_rows(got[n]) for n in ("conv_state", "ffn_state")]
    out += [s[None, None, 0:2] for s in states]
    for g in range(NG):
        v = np.asarray(got[f"s_kv{g}"])
        out.append(v.reshape(1, BATCH, v.shape[1], 2, HEADS, HEAD_DIM))
    out += [s[2:].reshape(2, BATCH, -1).transpose(1, 0, 2)[None] for s in states]
    return tuple(np.ascontiguousarray(o) for o in out)
```
